# Optimizing a Trainium2 kernel written in Bass

```python
import jax, jax.numpy as jnp
from jax import lax
import numpy as np

D_MODEL = 2048
BATCH = 1
SEQ = 256
DEPTH = 1

CHUNK = 64
D_MIX = D_MODEL
D_MLSTM = D_MIX // 2
MLSTM_HEADS = 4
MLSTM_HEAD_DIM = D_MLSTM // MLSTM_HEADS
D_LRU = D_MIX - D_MLSTM
LRU_BLOCKS = 8
LRU_BLOCK_DIM = D_LRU // LRU_BLOCKS
LRU_CONV = 4
LRU_C = 8.0
D_FF = 5632
FFN_CONV = 3
EPS = 1e-6
PROJ_COLS = 4 * D_MLSTM + 2 * MLSTM_HEADS + 2 * D_LRU

kernel_name = "hymba_mlstm_rglru_convffn"

def rmsnorm(x, g):
    xf = x.astype(jnp.float32)
    r = xf * lax.rsqrt(jnp.mean(xf * xf, axis=-1, keepdims=True) + EPS)
    return (r * g.astype(jnp.float32)).astype(x.dtype)

def causal_dwconv(x, w, b):
    K = w.shape[0]
    S = x.shape[1]
    xp = jnp.pad(x, ((0, 0), (K - 1, 0), (0, 0)))
    out = b + xp[:, 0:S, :] * w[0]
    for j in range(1, K):
        out = out + xp[:, j:j + S, :] * w[j]
    return out

def mlstm_chunkwise(q, k, v, i_pre, f_pre, head_g):
    B, S, H, dh = q.shape
    NC, L = S // CHUNK, CHUNK
    f32 = jnp.float32

    def to_chunks(t):
        t = t.astype(f32).reshape((B, NC, L, H) + t.shape[3:])
        return jnp.moveaxis(t, 3, 1)

    q = to_chunks(q) * (MLSTM_HEAD_DIM ** -0.5)
    k, v = to_chunks(k), to_chunks(v)
    ig = to_chunks(i_pre)
    logf = jax.nn.log_sigmoid(to_chunks(f_pre))
    b = jnp.cumsum(logf, axis=-1)
    b_tot = b[..., -1]

    w_end = b_tot[..., None] - b + ig
    m_loc = jnp.max(w_end, axis=-1)
    e_end = jnp.exp(w_end - m_loc[..., None])
    C_loc = jnp.einsum('bhcl,bhclk,bhclv->bhckv', e_end, k, v)
    n_loc = jnp.einsum('bhcl,bhclk->bhck', e_end, k)

    def step(carry, inp):
        C, n, m = carry
        bt, ml, Cl, nl = inp
        m_new = jnp.maximum(bt + m, ml)
        a = jnp.exp(bt + m - m_new)
        c = jnp.exp(ml - m_new)
        C_new = a[..., None, None] * C + c[..., None, None] * Cl
        n_new = a[..., None] * n + c[..., None] * nl
        return (C_new, n_new, m_new), (C, n, m)

    init = (jnp.zeros((B, H, dh, dh), f32), jnp.zeros((B, H, dh), f32), jnp.zeros((B, H), f32))
    xs = (jnp.moveaxis(b_tot, 2, 0), jnp.moveaxis(m_loc, 2, 0),
          jnp.moveaxis(C_loc, 2, 0), jnp.moveaxis(n_loc, 2, 0))
    _, (C_prev, n_prev, m_prev) = lax.scan(step, init, xs)
    C_prev = jnp.moveaxis(C_prev, 0, 2)
    n_prev = jnp.moveaxis(n_prev, 0, 2)
    m_prev = jnp.moveaxis(m_prev, 0, 2)

    causal = jnp.tril(jnp.ones((L, L), dtype=bool))
    D = b[..., :, None] - b[..., None, :] + ig[..., None, :]
    D = jnp.where(causal, D, -jnp.inf)
    m_inter = b + m_prev[..., None]
    m_t = jnp.maximum(m_inter, jnp.max(D, axis=-1))
    Wqk = jnp.einsum('bhctk,bhcsk->bhcts', q, k) * jnp.exp(D - m_t[..., None])
    e_inter = jnp.exp(m_inter - m_t)
    num = (jnp.einsum('bhcts,bhcsv->bhctv', Wqk, v)
           + e_inter[..., None] * jnp.einsum('bhctk,bhckv->bhctv', q, C_prev))
    den = jnp.sum(Wqk, axis=-1) + e_inter * jnp.einsum('bhctk,bhck->bhct', q, n_prev)
    h = num / jnp.maximum(jnp.abs(den), jnp.exp(-m_t))[..., None]

    h = h * lax.rsqrt(jnp.mean(h * h, axis=-1, keepdims=True) + EPS)
    h = h * head_g.astype(f32)[None, :, None, None, :]
    return jnp.moveaxis(h, 1, 3).reshape(B, S, H * dh)

def rglru(x_r, conv_w, conv_b, wa, ba, wx, bx, lam):
    B, S, _ = x_r.shape
    f32 = jnp.float32
    xc = causal_dwconv(x_r.astype(f32), conv_w.astype(f32), conv_b.astype(f32))
    xb = xc.reshape(B, S, LRU_BLOCKS, LRU_BLOCK_DIM)
    r = jax.nn.sigmoid(jnp.einsum('bsni,nij->bsnj', xb, wa.astype(f32)).reshape(B, S, D_LRU) + ba)
    i = jax.nn.sigmoid(jnp.einsum('bsni,nij->bsnj', xb, wx.astype(f32)).reshape(B, S, D_LRU) + bx)
    log_a = -LRU_C * r * jax.nn.softplus(-lam.astype(f32))
    a = jnp.exp(log_a)
    u = jnp.sqrt(-jnp.expm1(2.0 * log_a)) * (i * xc)

    def combine(e1, e2):
        a1, b1 = e1
        a2, b2 = e2
        return a1 * a2, a2 * b1 + b2

    _, h = lax.associative_scan(combine, (a, u), axis=1)
    return h

def setup_inputs(seed: int = 0) -> dict:
    key = jax.random.key(seed)
    ks = jax.random.split(key, 24)
    f32 = jnp.float32

    def nrm(k, shape, scale):
        return jax.random.normal(k, shape, f32) * scale

    x = jax.random.normal(ks[0], (BATCH, SEQ, D_MODEL), f32)
    norm_mix_g = 1.0 + nrm(ks[1], (DEPTH, D_MODEL), 0.02)
    w_in = nrm(ks[2], (DEPTH, D_MODEL, PROJ_COLS), D_MODEL ** -0.5)
    i_bias = nrm(ks[3], (DEPTH, MLSTM_HEADS), 0.1)
    f_bias = jnp.linspace(3.0, 6.0, MLSTM_HEADS, dtype=f32)[None, :] + nrm(ks[4], (DEPTH, MLSTM_HEADS), 0.1)
    b_gate_m = jnp.concatenate([i_bias, f_bias], axis=-1)
    mlstm_norm_g = 1.0 + nrm(ks[5], (DEPTH, MLSTM_HEADS, MLSTM_HEAD_DIM), 0.02)
    lru_conv_w = nrm(ks[6], (DEPTH, LRU_CONV, D_LRU), LRU_CONV ** -0.5)
    lru_conv_b = nrm(ks[7], (DEPTH, D_LRU), 0.01)
    lru_wa = nrm(ks[8], (DEPTH, LRU_BLOCKS, LRU_BLOCK_DIM, LRU_BLOCK_DIM), LRU_BLOCK_DIM ** -0.5)
    lru_ba = nrm(ks[9], (DEPTH, D_LRU), 0.01)
    lru_wx = nrm(ks[10], (DEPTH, LRU_BLOCKS, LRU_BLOCK_DIM, LRU_BLOCK_DIM), LRU_BLOCK_DIM ** -0.5)
    lru_bx = nrm(ks[11], (DEPTH, D_LRU), 0.01)
    u = jax.random.uniform(ks[12], (DEPTH, D_LRU), f32, 0.9, 0.999)
    a_base = u ** (1.0 / LRU_C)
    lru_lambda = jnp.log(a_base) - jnp.log1p(-a_base)
    w_out = nrm(ks[13], (DEPTH, D_MIX, D_MODEL), D_MIX ** -0.5)
    norm_ffn_g = 1.0 + nrm(ks[14], (DEPTH, D_MODEL), 0.02)
    w_up = nrm(ks[15], (DEPTH, D_MODEL, 2 * D_FF), D_MODEL ** -0.5)
    ffn_conv_w = nrm(ks[16], (DEPTH, FFN_CONV, D_FF), FFN_CONV ** -0.5)
    ffn_conv_b = nrm(ks[17], (DEPTH, D_FF), 0.01)
    w_down = nrm(ks[18], (DEPTH, D_FF, D_MODEL), D_FF ** -0.5)
    norm_final_g = 1.0 + nrm(ks[19], (D_MODEL,), 0.02)
    return {"x": x, "norm_mix_g": norm_mix_g, "w_in": w_in, "b_gate_m": b_gate_m,
            "mlstm_norm_g": mlstm_norm_g, "lru_conv_w": lru_conv_w, "lru_conv_b": lru_conv_b,
            "lru_wa": lru_wa, "lru_ba": lru_ba, "lru_wx": lru_wx, "lru_bx": lru_bx,
            "lru_lambda": lru_lambda, "w_out": w_out, "norm_ffn_g": norm_ffn_g, "w_up": w_up,
            "ffn_conv_w": ffn_conv_w, "ffn_conv_b": ffn_conv_b, "w_down": w_down,
            "norm_final_g": norm_final_g}

def reference(x, norm_mix_g, w_in, b_gate_m, mlstm_norm_g, lru_conv_w, lru_conv_b,
              lru_wa, lru_ba, lru_wx, lru_bx, lru_lambda, w_out, norm_ffn_g, w_up,
              ffn_conv_w, ffn_conv_b, w_down, norm_final_g):
    B, S, _ = x.shape
    H, dh = MLSTM_HEADS, MLSTM_HEAD_DIM
    split_at = [D_MLSTM, 2 * D_MLSTM, 3 * D_MLSTM, 4 * D_MLSTM,
                4 * D_MLSTM + 2 * H, 4 * D_MLSTM + 2 * H + D_LRU]
    for l in range(DEPTH):
        n1 = rmsnorm(x, norm_mix_g[l])
        proj = n1 @ w_in[l]
        q, k, v, o_pre, if_pre, x_r, g_r = jnp.split(proj, split_at, axis=-1)
        if_pre = if_pre.astype(jnp.float32) + b_gate_m[l].astype(jnp.float32)
        i_pre, f_pre = if_pre[..., :H], if_pre[..., H:]
        h_m = mlstm_chunkwise(q.reshape(B, S, H, dh), k.reshape(B, S, H, dh),
                              v.reshape(B, S, H, dh), i_pre, f_pre, mlstm_norm_g[l])
        h_m = jax.nn.sigmoid(o_pre.astype(jnp.float32)) * h_m
        h_r = rglru(x_r, lru_conv_w[l], lru_conv_b[l], lru_wa[l], lru_ba[l],
                    lru_wx[l], lru_bx[l], lru_lambda[l])
        h_r = h_r * jax.nn.gelu(g_r.astype(jnp.float32))
        mix = jnp.concatenate([h_m, h_r], axis=-1).astype(x.dtype)
        x = x + mix @ w_out[l]
        n2 = rmsnorm(x, norm_ffn_g[l])
        gate, up = jnp.split(n2 @ w_up[l], 2, axis=-1)
        gate = causal_dwconv(gate, ffn_conv_w[l], ffn_conv_b[l])
        x = x + (jax.nn.silu(gate) * up) @ w_down[l]
    return rmsnorm(x, norm_final_g)


_drawn_inputs = setup_inputs


def setup_inputs(seed=0):
    import zlib

    import numpy as np

    out = dict(_drawn_inputs(seed))
    spreads = {}
    factors = {'norm_mix_g': 3.001,
     'mlstm_norm_g': 18.877,
     'lru_conv_b': 3.18,
     'lru_ba': 39.115,
     'lru_bx': 29.799,
     'norm_ffn_g': 3.978,
     'ffn_conv_b': 24.074,
     'norm_final_g': 8.469}
    for name, (base, spread) in spreads.items():
        noise = np.random.default_rng([zlib.crc32(name.encode()), seed]).standard_normal(out[name].shape)
        drawn = base * np.exp(spread * noise) if base else spread * noise
        out[name] = __import__('jax').numpy.asarray(drawn.astype(out[name].dtype))
    for name, factor in factors.items():
        out[name] = (out[name] * factor).astype(out[name].dtype)
    return out
```

```python
from contextlib import ExitStack

import concourse.bass as bass
from concourse import mybir

F32 = mybir.dt.float32
F32R = mybir.dt.float32r
ALU = mybir.AluOpType
ACT = mybir.ActivationFunctionType

P = 128
D = 2048
S = 256
KT = D // P
ROWS = S // P
H = 4
DH = 256
D_M = H * DH
D_L = D - D_M
LBLK = D_L // P
TAPS = 4
D_FF = 5632
FT = D_FF // P
FTAPS = 3
EPS = 1e-6
LRU_C = 8.0

RING = 4
CH = 4
COLS = 256
HALF = CH * COLS
BANK = 512

MIX_GROUPS = 6
OUT_BODIES = KT // RING
UP_ITERS = D_FF // COLS
DOWN_BODIES = FT // RING
G_MIX = 0
G_OUT = G_MIX + H * MIX_GROUPS
G_UP = G_OUT + 2 * OUT_BODIES
G_DOWN = G_UP + 2 * UP_ITERS
G_END = G_DOWN + 2 * DOWN_BODIES

NOT_BANKED = 2 * OUT_BODIES
FREE_AT_START = 2

PAR_GMIX = 0
PAR_GFFN = PAR_GMIX + KT
PAR_HEAD = PAR_GFFN + KT
PAR_LRU = PAR_HEAD + 2 * H
LRU_PAR = 8
PAR_FFN = PAR_LRU + LBLK * LRU_PAR
FFN_PAR = 4
PAR_GATE = PAR_FFN + FT * FFN_PAR
NPAR = PAR_GATE + 1
F_ROW = 32

C_ID, C_TRI, C_ONE, C_SEL = 0, P, 2 * P, 3 * P
NCONST = C_SEL + H * P


class Steps:

    def __init__(self, sem, base, names):
        self.sem, self.base, self.names = sem, base, names.split()
        self.n = len(self.names)

    def after(self, name, i=0):
        return i * self.n + (self.base + self.names.index(name) + 1)

    def end(self, iterations=1):
        return self.base + self.n * iterations


def hybrid_block(nc, x, w_in, w_out, w_up, w_down, wa, wx, gate_w, par_in, const_in, gfin_in, out):
    with ExitStack() as ctx:
        def sem(name):
            return ctx.enter_context(nc.semaphore(name))

        def sb(name, shape, dt=F32, where=ctx):
            return where.enter_context(nc.sbuf_tensor(name, shape, dt))

        xres = sb("xres", [P, ROWS, D])
        xn = sb("xn", [P, ROWS, D])
        xT = sb("xT", [P, KT, 2, S], F32R)
        raw = sb("raw", [P, RING, HALF])
        w = sb("w", [P, RING, CH, 2, COLS], F32R)
        aT = sb("aT", [P, RING, 2, S], F32R)
        par = sb("par", [P, NPAR])
        cst = sb("cst", [P, NCONST])
        gfin = sb("gfin", [P, D])
        small = sb("small", [P, 16])
        ident = cst[:, C_ID:C_ID + P]
        tri = cst[:, C_TRI:C_TRI + P]
        ones = cst[:, C_ONE:C_ONE + P]

        gw = gfin[:].rearrange("p (k n) -> p k n", k=KT)
        gate_cols = ExitStack()
        gwh = sb("gwh", [P, KT, P], F32R, where=gate_cols)
        gwl = sb("gwl", [P, KT, P], F32R, where=gate_cols)
        gate_cols.close()
        mixer = ExitStack()
        mixT = sb("mixT", [P, KT, S], where=mixer)
        qT = sb("qT", [P, 2, S], where=mixer)
        kT = sb("kT", [P, 2, S], where=mixer)
        vN = sb("vN", [P, ROWS, DH], where=mixer)
        negM = sb("negM", [P, H, S], where=mixer)
        floor = sb("floor", [P, H, S], where=mixer)
        gcol = sb("gcol", [P, ROWS, H], where=mixer)
        decay = sb("decay", [P, 3 * P], where=mixer)
        pT = sb("pT", [P, 3 * P], where=mixer)
        rden = sb("rden", [P, S], where=mixer)
        hT = sb("hT", [P, 2, S], where=mixer)
        hsq = sb("hsq", [P, 2, S], where=mixer)
        oT = sb("oT", [P, 2, S], where=mixer)
        rstd_h = sb("rstd_h", [P, S], where=mixer)
        xr = sb("xr", [P, 2, S + TAPS - 1], where=mixer)
        xc = sb("xc", [P, 2, S], where=mixer)
        rg = sb("rg", [P, 2, S], where=mixer)
        ig = sb("ig", [P, 2, S], where=mixer)
        lruA = sb("lruA", [P, 2, S], where=mixer)
        lruT = sb("lruT", [P, 2, S], where=mixer)
        lruU = sb("lruU", [P, 2, S], where=mixer)
        lruH = sb("lruH", [P, 2, S], where=mixer)
        gr = sb("gr", [P, 2, S], where=mixer)
        gr2 = sb("gr2", [P, 2, S], where=mixer)
        lru_w = sb("lru_w", [P, 2, 2, P], where=mixer)
        lp = sb("lp", [P, 4, LBLK], where=mixer)
        hg = sb("hg", [P, 2 * H], where=mixer)
        gates = ExitStack()
        grow = sb("grow", [64, S], where=gates)
        gtmp = sb("gtmp", [64, S], where=gates)
        logf = sb("logf", [H, S], where=gates)
        fsum = sb("fsum", [H, S], where=gates)
        gdif = sb("gdif", [H, S], where=gates)
        neg = sb("neg", [H, 2, S], where=gates)
        gates.close()
        mixer.close()
        ffn = ExitStack()
        act = sb("act", [P, FT, S], where=ffn)
        fg = sb("fg", [P, 2, S + FTAPS - 1], where=ffn)
        fc = sb("fc", [P, 2, S], where=ffn)
        fs = sb("fs", [P, 2, S], where=ffn)
        fu = sb("fu", [P, 2, S], where=ffn)
        ffn.close()

        ps = ctx.enter_context(nc.psum_tensor("ps", [P, 8, BANK], F32))
        B_SC, B_R, B_PV, B_DEN = 4, 5, 6, 7
        B_I = B_SC

        x_landed = sem("x_landed")
        par_landed = sem("par_landed")
        gate_landed = sem("gate_landed")
        gfin_landed = sem("gfin_landed")
        lru_w_landed = sem("lru_w_landed")
        raw_landed = [sem(f"raw_landed{s}") for s in range(RING)]
        hi_ready = sem("hi_ready")
        lo_ready = sem("lo_ready")
        unit_used = sem("unit_used")
        group_free = sem("group_free")
        half_copied = sem("half_copied")
        a_hi_ready = sem("a_hi_ready")
        a_lo_ready = sem("a_lo_ready")
        stored = sem("stored")
        act_step, dve_step, pe_step, pool_step = sem("act_step"), sem("dve_step"), sem("pe_step"), sem("pool_step")

        norm_act = " ".join([f"sq{r}" for r in range(ROWS)] + ["std"])
        norm_dve = " ".join(["var", "rstd"] + [f"xn{r}_{c}" for c in range(4) for r in range(ROWS)])
        tr_steps = " ".join(f"t{b}" for b in range(KT // 2))
        A0 = Steps(act_step, 0, norm_act + " " + tr_steps + " gw_hi lam_exp lam_ln gate_half f_exp f_ln floor0 floor1 floor2 floor3")
        V0 = Steps(dve_step, 0, "start " + norm_dve + " " + tr_steps + " gw_lo lam_abs1 lam_abs2 lam_relu lp_c lp_nc lp_b hg"
                   " gate_sum gate_bias f_neg f_abs logf fsum gdif cmax neg1 neg2 gcol0 gcol1"
                   " negM0 negM1 negM2 negM3 pads")
        E0 = Steps(pe_step, 0, tr_steps + " gates gcol0 gcol1 bc0 bc1 bc2 bc3")
        A1 = Steps(act_step, A0.end(), "decay hsq rms_std o_tanh r_tanh0 r_tanh1 i_tanh0 i_tanh1 lru_a0 lru_a1 lru_t0 lru_t1 lru_s g_tanh")
        V1 = Steps(dve_step, V0.end(), "arg0 arg1 pT dneg den rden hT"
                   " conv0_0 conv1_0 conv0_1 conv1_1 conv0_2 conv1_2 conv0_3 conv1_3 rstd og mix0 mix1"
                   " ux t1 rt w u scan0 scan1 gsq gp gq gh mixl")
        E1 = Steps(pe_step, E0.end(), "scores pv rms lru")
        L1 = Steps(pool_step, 0, "mask0 mask1")
        A2 = Steps(act_step, A1.end(H), norm_act + " " + tr_steps)
        V2 = Steps(dve_step, V1.end(H), "out0_0 out0_1 out1_0 out1_1 " + norm_dve + " " + tr_steps + " fpad")
        E2 = Steps(pe_step, E1.end(H), tr_steps)
        A3 = Steps(act_step, A2.end(), "silu")
        V3 = Steps(dve_step, V2.end(), "c0_0 c1_0 c0_1 c1_1 c0_2 c1_2 act")
        A4 = Steps(act_step, A3.end(UP_ITERS), "sq0 sq1 std")
        V4 = Steps(dve_step, V3.end(UP_ITERS), "out0_0 out0_1 out1_0 out1_1 var rstd " + " ".join(f"y{r}_{c}" for r in range(ROWS) for c in range(2)))

        def freed(n):
            return n + (1 + FREE_AT_START)

        def after(eng, steps, name, i=0):
            eng.wait_ge(steps.sem, steps.after(name, i))

        def did(ins, steps, name, seen={}):
            key = id(steps)
            assert steps.names[seen.get(key, 0) % steps.n] == name, (name, steps.names[seen.get(key, 0) % steps.n])
            seen[key] = seen.get(key, 0) + 1
            ins.then_inc(steps.sem, 1)

        block = ctx.enter_context(nc.Block())

        @block.sync
        def _(sp):
            xv = x.rearrange("a (r p) d -> (a r) p d", p=P)
            for r in range(ROWS):
                sp.dma_start(xres[:, r, :], xv[r]).then_inc(x_landed, 16)

            def load(group, s, src, dst):
                sp.wait_ge(lo_ready, group * RING + s + 1)
                sp.dma_start(dst, src).then_inc(raw_landed[s], 16)

            in_v = w_in.rearrange("(s c p) n -> s p c n", c=CH, p=P)
            up_v = w_up.rearrange("(s c p) n -> s p c n", c=CH, p=P)

            def load_group(group, view, col):
                for s in range(RING):
                    load(group, s, view[s, :, :, bass.ds(col, COLS)],
                         raw[:, s, :].rearrange("p (c n) -> p c n", c=CH))

            def load_body(group, weights, b, half):
                rows = weights.rearrange("(b s p) n -> s p b n", s=RING, p=P)
                for s in range(RING):
                    load(group, s, rows[s, :, bass.ds(b, 1), half * HALF:(half + 1) * HALF],
                         raw[:, s, :].rearrange("p (b n) -> p b n", b=1))

            first_cols = [0, D_M, 2 * D_M, 3 * D_M, 4 * D_M + 2 * H, 4 * D_M + 2 * H + D_L]
            wa_v = wa.rearrange("(i b) k j -> i k b j", b=2)
            wx_v = wx.rearrange("(i b) k j -> i k b j", b=2)
            with sp.Fori(0, H) as i:
                for g, col in enumerate(first_cols):
                    load_group(i * MIX_GROUPS + (G_MIX + g), in_v, i * COLS + col)
                    if g == 1:
                        sp.wait_ge(pe_step, E1.after("lru", i - 1))
                        for n, view in enumerate((wa_v, wx_v)):
                            sp.dma_start(lru_w[:, :, n, :], view[bass.ds(i, 1)].rearrange("i k b j -> k (i b) j")).then_inc(lru_w_landed, 16)
            for half in range(2):
                with sp.Fori(0, OUT_BODIES) as b:
                    load_body(b + (G_OUT + half * OUT_BODIES), w_out, b, half)
            with sp.Fori(0, UP_ITERS) as j:
                for g in range(2):
                    load_group(j * 2 + (G_UP + g), up_v, j * COLS + g * D_FF)
            for half in range(2):
                with sp.Fori(0, DOWN_BODIES) as b:
                    load_body(b + (G_DOWN + half * DOWN_BODIES), w_down, b, half)
            yv = out.rearrange("a (r p) (c d) -> (a r) c p d", p=P, c=2)
            for r in range(ROWS):
                for c in range(2):
                    after(sp, V4, f"y{r}_{c}")
                    sp.dma_start(yv[r, c], xn[:, r, c * HALF:(c + 1) * HALF]).then_inc(stored, 16)
            sp.wait_ge(stored, 16 * ROWS * 2)

        @block.scalar
        def _(act_e):
            sc = nc.scalar

            def act_fn(out_, in_, fn=ACT.Copy, **kw):
                return sc.activation(out_, in_, fn, **kw)

            def round_units(group, slots=range(RING)):
                for s in slots:
                    act_e.wait_ge(raw_landed[s], group * 16 + 16)
                    act_e.wait_ge(unit_used, group * RING + s + 1)
                    act_fn(w[:, s, :, 0, :], raw[:, s, :].rearrange("p (c n) -> p c n", c=CH)).then_inc(hi_ready, 1)

            def round_tiles(src, first):
                for s in range(RING):
                    act_fn(aT[:, s, 0, :], src[:, bass.ds(first + s, 1), :].rearrange("p a n -> p (a n)")).then_inc(a_hi_ready, 1)

            def copy_half(group, pair, dst):
                act_e.wait_ge(unit_used, group * RING + 2 * RING)
                act_fn(dst, ps[:, 2 * pair:2 * pair + 2, 0:COLS]).then_inc(half_copied, 1)

            def norm_stats(A, V, name_in=None):
                if name_in is None:
                    act_e.wait_ge(x_landed, 16 * ROWS)
                for r in range(ROWS):
                    if name_in is not None:
                        after(act_e, V, f"{name_in}{r}")
                    did(act_fn(xn[:, r, :], xres[:, r, :], ACT.Square, accum_out=small[:, r:r + 1]), A, f"sq{r}")
                after(act_e, V, "var")
                did(act_fn(small[:, 4:6], small[:, 2:4], ACT.Sqrt), A, "std")

            def transposed_hi(A, E, gains):
                for b in range(KT // 2):
                    after(act_e, E, f"t{b}")
                    for n in range(2):
                        kt = 2 * b + n
                        ins = act_fn(xT[:, kt, 0, :], ps[:, 4 + b % 4, n * S:(n + 1) * S],
                                     scale=par[:, gains + kt:gains + kt + 1])
                    did(ins, A, f"t{b}")

            after(act_e, V0, "start")
            norm_stats(A0, V0)
            round_units(G_MIX)
            act_e.wait_ge(par_landed, 32)
            transposed_hi(A0, E0, PAR_GMIX)
            act_e.wait_ge(gate_landed, 16)
            did(act_fn(gwh[:], gw), A0, "gw_hi")
            after(act_e, V0, "lam_abs2")
            did(act_fn(lp[:, 2, :], lp[:, 2, :], ACT.Exp), A0, "lam_exp")
            after(act_e, A0, "lam_exp")
            did(act_fn(lp[:, 2, :], lp[:, 2, :], ACT.Ln, bias=1.0), A0, "lam_ln")
            after(act_e, E0, "gates")
            did(act_fn(grow[:], ps[0:64, B_SC, 0:S]), A0, "gate_half")
            after(act_e, V0, "f_abs")
            did(act_fn(gtmp[F_ROW:F_ROW + H], gtmp[F_ROW:F_ROW + H], ACT.Exp), A0, "f_exp")
            after(act_e, A0, "f_exp")
            did(act_fn(gtmp[F_ROW:F_ROW + H], gtmp[F_ROW:F_ROW + H], ACT.Ln, bias=1.0), A0, "f_ln")
            for h in range(H):
                after(act_e, E0, f"bc{h}")
                did(act_fn(floor[:, h, :], ps[:, 4 + h, S:2 * S], ACT.Exp), A0, f"floor{h}")

            with act_e.Fori(0, H) as i:
                g0 = i * MIX_GROUPS + G_MIX
                round_units(g0 + 1)
                act_e.wait_ge(pe_step, E1.after("scores", i - 1))
                copy_half(g0, 0, qT[:])
                after(act_e, V1, "arg1", i)
                did(act_fn(decay[:], decay[:], ACT.Exp), A1, "decay")
                round_units(g0 + 2)
                copy_half(g0 + 1, 1, kT[:])
                round_units(g0 + 3)
                act_e.wait_ge(pe_step, E1.after("pv", i - 1))
                copy_half(g0 + 2, 0, vN[:])
                round_units(g0 + 4)
                copy_half(g0 + 3, 1, oT[:])
                after(act_e, V1, "hT", i)
                did(act_fn(hsq[:], hT[:], ACT.Square), A1, "hsq")
                round_units(g0 + 5)
                after(act_e, E1, "rms", i)
                did(act_fn(rstd_h[:], ps[:, B_DEN, S:2 * S], ACT.Sqrt, scale=1.0 / DH, bias=small[:, 8:9]), A1, "rms_std")
                copy_half(g0 + 4, 0, xr[:, :, TAPS - 1:])
                act_e.wait_ge(group_free, freed(g0 + 3))
                did(act_fn(oT[:], oT[:], ACT.Tanh, scale=0.5), A1, "o_tanh")
                round_units(g0 + 6, range(3))
                after(act_e, E1, "lru", i)
                for n in range(2):
                    did(act_fn(rg[:, n, :], ps[:, B_R, n * S:(n + 1) * S], ACT.Tanh, scale=0.5,
                               bias=lp[:, 0, bass.ds(i * 2 + n, 1)]), A1, f"r_tanh{n}")
                for n in range(2):
                    did(act_fn(ig[:, n, :], ps[:, B_I, n * S:(n + 1) * S], ACT.Tanh, scale=0.5,
                               bias=lp[:, 1, bass.ds(i * 2 + n, 1)]), A1, f"i_tanh{n}")
                after(act_e, A1, "r_tanh1", i)
                for n in range(2):
                    did(act_fn(lruA[:, n, :], rg[:, n, :], ACT.Exp, scale=lp[:, 2, bass.ds(i * 2 + n, 1)],
                               bias=lp[:, 2, bass.ds(i * 2 + n, 1)]), A1, f"lru_a{n}")
                for n in range(2):
                    did(act_fn(lruT[:, n, :], rg[:, n, :], ACT.Tanh, scale=lp[:, 3, bass.ds(i * 2 + n, 1)],
                               bias=lp[:, 3, bass.ds(i * 2 + n, 1)]), A1, f"lru_t{n}")
                after(act_e, V1, "w", i)
                did(act_fn(lruT[:], lruT[:], ACT.Sqrt, scale=0.5), A1, "lru_s")
                round_units(g0 + 6, range(3, RING))
                copy_half(g0 + 5, 1, gr[:])
                after(act_e, V1, "gq", i)
                did(act_fn(gr2[:], gr2[:], ACT.Tanh, scale=0.7978845608028654), A1, "g_tanh")

            def contraction(src, first_group, bodies):
                for half in range(2):
                    base = first_group + half * bodies + 1
                    with act_e.Fori(0, bodies - 1) as b:
                        round_units(b + base)
                        round_tiles(src, b * RING + RING)
                    if base + bodies - 1 < G_END:
                        round_units(base + bodies - 1)
                    if half == 0:
                        round_tiles(src, 0)

            after(act_e, V1, "mix1", H - 1)
            round_tiles(mixT, 0)
            after(act_e, V1, "mixl", H - 1)
            contraction(mixT, G_OUT, OUT_BODIES)
            norm_stats(A2, V2, "out1_")
            transposed_hi(A2, E2, PAR_GFFN)

            with act_e.Fori(0, UP_ITERS) as j:
                g0 = j * 2 + G_UP
                round_units(g0 + 1)
                copy_half(g0, 0, fg[:, :, FTAPS - 1:])
                after(act_e, V3, "c1_2", j)
                did(act_fn(fs[:], fc[:], ACT.Silu), A3, "silu")
                round_units(g0 + 2)
                act_e.wait_ge(dve_step, V3.after("act", j - 1))
                copy_half(g0 + 1, 1, fu[:])

            round_tiles(act, 0)
            after(act_e, V3, "act", UP_ITERS - 1)
            contraction(act, G_DOWN, DOWN_BODIES)
            norm_stats(A4, V4, "out1_")

        @block.vector
        def _(dve):
            v = nc.vector

            def split_units(group, slots=range(RING)):
                for s in slots:
                    dve.wait_ge(hi_ready, group * RING + s + 1)
                    v.tensor_tensor(w[:, s, :, 1, :], raw[:, s, :].rearrange("p (c n) -> p c n", c=CH),
                                    w[:, s, :, 0, :], ALU.subtract).then_inc(lo_ready, 1)

            def split_tiles(src, first, count):
                for s in range(RING):
                    dve.wait_ge(a_hi_ready, count + s + 1)
                    v.tensor_tensor(aT[:, s, 1, :], src[:, bass.ds(first + s, 1), :].rearrange("p a n -> p (a n)"),
                                    aT[:, s, 0, :], ALU.subtract).then_inc(a_lo_ready, 1)

            def add_half(n, pair, dst):
                dve.wait_ge(half_copied, n + 1)
                v.tensor_tensor(dst, ps[:, 2 * pair:2 * pair + 2, COLS:2 * COLS], dst, ALU.add).then_inc(group_free, 1)

            def norm_scale(A, V, S_sq="sq1"):
                after(dve, A, S_sq)
                did(v.tensor_scalar(small[:, 2:4], small[:, 0:2], 1.0 / D, EPS, ALU.mult, ALU.add), V, "var")
                after(dve, A, "std")
                did(v.reciprocal(small[:, 6:8], small[:, 4:6]), V, "rstd")
                after(dve, V, "rstd")

            def normalise(A, V):
                norm_scale(A, V)
                for c in range(4):
                    for r in range(ROWS):
                        cols = slice(c * BANK, (c + 1) * BANK)
                        did(v.tensor_scalar(xn[:, r, cols], xres[:, r, cols], small[:, 6 + r:7 + r], None, ALU.mult),
                            V, f"xn{r}_{c}")

            def transposed_lo(A, V, gains):
                for b in range(KT // 2):
                    after(dve, A, f"t{b}")
                    for n in range(2):
                        kt = 2 * b + n
                        ins = v.scalar_tensor_tensor(out=xT[:, kt, 1, :], in0=ps[:, 4 + b % 4, n * S:(n + 1) * S],
                                                     scalar=par[:, gains + kt:gains + kt + 1], in1=xT[:, kt, 0, :],
                                                     op0=ALU.mult, op1=ALU.subtract)
                    did(ins, V, f"t{b}")

            v.memset(small[:], 0.0).then_inc(lo_ready, RING)
            dve.wait_ge(lo_ready, RING)
            v.memset(small[:, 9:10], 0.0).then_inc(group_free, FREE_AT_START)
            did(v.memset(small[:, 8:9], EPS), V0, "start")
            normalise(A0, V0)
            split_units(G_MIX)
            dve.wait_ge(par_landed, 32)
            transposed_lo(A0, V0, PAR_GMIX)
            after(dve, A0, "gw_hi")
            did(v.tensor_tensor(gwl[:], gw, gwh[:], ALU.subtract), V0, "gw_lo")

            lru_par = par[:, PAR_LRU:PAR_LRU + LBLK * LRU_PAR].rearrange("p (b n) -> p n b", n=LRU_PAR)
            lam = lru_par[:, 7, :]
            did(v.tensor_scalar(lp[:, 3, :], lam, -1.0, None, ALU.mult), V0, "lam_abs1")
            after(dve, V0, "lam_abs1")
            did(v.tensor_tensor(lp[:, 2, :], lp[:, 3, :], lam, ALU.min), V0, "lam_abs2")
            after(dve, V0, "lam_abs2")
            did(v.tensor_scalar(lp[:, 3, :], lp[:, 3, :], 0.0, None, ALU.max), V0, "lam_relu")
            after(dve, A0, "lam_ln")
            after(dve, V0, "lam_relu")
            did(v.tensor_tensor(lp[:, 3, :], lp[:, 3, :], lp[:, 2, :], ALU.add), V0, "lp_c")
            after(dve, V0, "lp_c")
            v.tensor_scalar(lp[:, 2, :], lp[:, 3, :], -LRU_C / 2, None, ALU.mult)
            did(v.tensor_scalar(lp[:, 0:2, :], lru_par[:, 5:7, :], 0.5, None, ALU.mult), V0, "lp_nc")
            after(dve, V0, "lp_nc")
            did(v.tensor_scalar(lp[:, 3, :], lp[:, 3, :], LRU_C / 2, None, ALU.mult), V0, "lp_b")
            did(v.tensor_scalar(hg[:], par[:, PAR_HEAD:PAR_HEAD + 2 * H], 0.5, None, ALU.mult), V0, "hg")

            frow = slice(F_ROW, F_ROW + H)
            after(dve, A0, "gate_half")
            did(v.tensor_tensor(grow[:], ps[0:64, B_SC, S:2 * S], grow[:], ALU.add), V0, "gate_sum")
            after(dve, V0, "gate_sum")
            did(v.tensor_scalar(grow[:], grow[:], par[0:64, PAR_GATE:PAR_GATE + 1], None, ALU.add), V0, "gate_bias")
            after(dve, V0, "gate_bias")
            did(v.tensor_scalar(gtmp[frow], grow[frow], -1.0, None, ALU.mult), V0, "f_neg")
            after(dve, V0, "f_neg")
            did(v.tensor_tensor(gtmp[frow], gtmp[frow], grow[frow], ALU.min), V0, "f_abs")
            after(dve, A0, "f_ln")
            did(v.scalar_tensor_tensor(out=logf[:], in0=grow[frow], scalar=0.0, in1=gtmp[frow],
                                       op0=ALU.min, op1=ALU.subtract), V0, "logf")
            after(dve, V0, "logf")
            one_row = cst[0:H, C_ONE:C_ONE + 1].to_broadcast([H, S])
            did(v.tensor_tensor_scan(fsum[:], one_row, logf[:], 0.0, ALU.mult, ALU.add), V0, "fsum")
            after(dve, V0, "fsum")
            did(v.tensor_tensor(gdif[:], grow[0:H], fsum[:], ALU.subtract), V0, "gdif")
            after(dve, V0, "gdif")
            did(v.tensor_tensor_scan(logf[:], one_row, gdif[:], 0.0, ALU.mult, ALU.max), V0, "cmax")
            after(dve, V0, "cmax")
            did(v.tensor_scalar(neg[:, 0, :], logf[:], -1.0, None, ALU.mult), V0, "neg1")
            after(dve, V0, "neg1")
            did(v.tensor_tensor(neg[:, 1, :], neg[:, 0, :], fsum[:], ALU.subtract), V0, "neg2")
            for r in range(ROWS):
                after(dve, E0, f"gcol{r}")
                did(v.tensor_copy(gcol[:, r, :], ps[:, 5 + r, 0:H]), V0, f"gcol{r}")
            for h in range(H):
                after(dve, A0, f"floor{h}")
                did(v.tensor_copy(negM[:, h, :], ps[:, 4 + h, 0:S]), V0, f"negM{h}")
            did(v.memset(xr[:, :, 0:TAPS - 1], 0.0), V0, "pads")
            after(dve, V0, "pads")

            with dve.Fori(0, H) as i:
                g0 = i * MIX_GROUPS + G_MIX

                def lpar(n, k):
                    return par[:, bass.ds(i * (2 * LRU_PAR) + (PAR_LRU + n * LRU_PAR + k), 1)]

                def chain(name):
                    after(dve, V1, name, i)

                split_units(g0 + 1)
                add_half(g0, 0, qT[:])
                dve.wait_ge(dve_step, V1.after("pT", i - 1))
                minus_m = negM[:, bass.ds(i, 1), :].rearrange("p a t -> p (a t)")
                did(v.tensor_scalar(decay[:, 0:S], minus_m, gcol[:, 0, bass.ds(i, 1)], 0.0, ALU.add, ALU.min), V1, "arg0")
                did(v.tensor_scalar(decay[:, S:S + P], negM[:, bass.ds(i, 1), P:S].rearrange("p a t -> p (a t)"),
                                    gcol[:, 1, bass.ds(i, 1)], 0.0, ALU.add, ALU.min), V1, "arg1")
                split_units(g0 + 2)
                add_half(g0 + 1, 1, kT[:])
                split_units(g0 + 3)
                add_half(g0 + 2, 0, vN[:])
                after(dve, L1, "mask1", i)
                after(dve, E1, "scores", i)
                did(v.scalar_tensor_tensor(out=pT[:], in0=ps[:, B_SC, 0:3 * P], scalar=DH ** -0.5, in1=decay[:],
                                           op0=ALU.mult, op1=ALU.mult), V1, "pT")
                split_units(g0 + 4)
                add_half(g0 + 3, 1, oT[:])
                after(dve, E1, "pv", i)
                did(v.scalar_tensor_tensor(out=rden[:], in0=ps[:, B_DEN, 0:S], scalar=-1.0,
                                           in1=floor[:, bass.ds(i, 1), :].rearrange("p a t -> p (a t)"),
                                           op0=ALU.mult, op1=ALU.max), V1, "dneg")
                chain("dneg")
                did(v.tensor_tensor(rden[:], ps[:, B_DEN, 0:S], rden[:], ALU.max), V1, "den")
                chain("den")
                did(v.reciprocal(rden[:], rden[:]), V1, "rden")
                chain("rden")
                did(v.tensor_tensor(hT[:], ps[:, B_PV, :].rearrange("p (a t) -> p a t", a=2),
                                    rden[:].unsqueeze(1).to_broadcast([P, 2, S]), ALU.mult), V1, "hT")
                split_units(g0 + 5)
                add_half(g0 + 4, 0, xr[:, :, TAPS - 1:])
                dve.wait_ge(group_free, freed(g0 + 4))
                for k in range(TAPS):
                    for n in range(2):
                        tap = xr[:, n, k:k + S]
                        if k == 0:
                            did(v.tensor_scalar(xc[:, n, :], tap, lpar(n, k), lpar(n, TAPS), ALU.mult, ALU.add),
                                V1, f"conv{n}_{k}")
                        else:
                            chain(f"conv{n}_{k - 1}")
                            did(v.scalar_tensor_tensor(out=xc[:, n, :], in0=tap, scalar=lpar(n, k), in1=xc[:, n, :],
                                                       op0=ALU.mult, op1=ALU.add), V1, f"conv{n}_{k}")
                after(dve, A1, "rms_std", i)
                did(v.reciprocal(rstd_h[:], rstd_h[:]), V1, "rstd")
                after(dve, A1, "o_tanh", i)
                did(v.scalar_tensor_tensor(out=hT[:], in0=oT[:], scalar=1.0, in1=hT[:], op0=ALU.add, op1=ALU.mult), V1, "og")
                chain("og")
                for n in range(2):
                    did(v.scalar_tensor_tensor(out=mixT[:, bass.ds(i * 2 + n, 1), :].rearrange("p a t -> p (a t)"),
                                               in0=hT[:, n, :], scalar=hg[:, bass.ds(i * 2 + n, 1)], in1=rstd_h[:],
                                               op0=ALU.mult, op1=ALU.mult), V1, f"mix{n}")
                split_units(g0 + 6, range(3))
                after(dve, A1, "i_tanh1", i)
                did(v.scalar_tensor_tensor(out=lruU[:], in0=ig[:], scalar=1.0, in1=xc[:], op0=ALU.add, op1=ALU.mult), V1, "ux")
                after(dve, A1, "lru_t1", i)
                did(v.tensor_scalar(lruH[:], lruT[:], 1.0, None, ALU.add), V1, "t1")
                chain("t1")
                did(v.reciprocal(lruH[:], lruH[:]), V1, "rt")
                chain("rt")
                did(v.tensor_tensor(lruT[:], lruT[:], lruH[:], ALU.mult), V1, "w")
                split_units(g0 + 6, range(3, RING))
                after(dve, A1, "lru_s", i)
                did(v.tensor_tensor(lruU[:], lruU[:], lruT[:], ALU.mult), V1, "u")
                chain("u")
                for n in range(2):
                    did(v.tensor_tensor_scan(lruH[:, n, :], lruA[:, n, :], lruU[:, n, :], 0.0, ALU.mult, ALU.add),
                        V1, f"scan{n}")
                add_half(g0 + 5, 1, gr[:])
                dve.wait_ge(group_free, freed(g0 + 5))
                did(v.tensor_tensor(gr2[:], gr[:], gr[:], ALU.mult), V1, "gsq")
                chain("gsq")
                did(v.tensor_scalar(gr2[:], gr2[:], 0.044715, 1.0, ALU.mult, ALU.add), V1, "gp")
                chain("gp")
                did(v.tensor_tensor(gr2[:], gr2[:], gr[:], ALU.mult), V1, "gq")
                after(dve, A1, "g_tanh", i)
                did(v.scalar_tensor_tensor(out=gr2[:], in0=gr2[:], scalar=1.0, in1=gr[:], op0=ALU.add, op1=ALU.mult), V1, "gh")
                chain("gh")
                did(v.scalar_tensor_tensor(out=mixT[:, bass.ds(i * 2 + 2 * H, 2), :], in0=gr2[:], scalar=0.5, in1=lruH[:],
                                           op0=ALU.mult, op1=ALU.mult), V1, "mixl")

            def add_residual(V, half):
                for r in range(ROWS):
                    cols = slice(half * HALF, (half + 1) * HALF)
                    bank = 4 * (1 - half) + 2 * r
                    did(v.tensor_tensor(xres[:, r, cols], ps[:, bank:bank + 2, :].rearrange("p a n -> p (a n)"),
                                        xres[:, r, cols], ALU.add), V, f"out{half}_{r}")

            def contraction(src, first_group, bodies, count, V):
                for half in range(2):
                    base = first_group + half * bodies + 1
                    tiles = count + half * bodies * RING + RING
                    if half == 1:
                        split_units(base)
                        split_tiles(src, RING, tiles)
                        dve.wait_ge(unit_used, base * RING)
                        add_residual(V, 0)
                    with dve.Fori(half, bodies - 1) as b:
                        split_units(b + base)
                        split_tiles(src, b * RING + RING, b * RING + tiles)
                    if base + bodies - 1 < G_END:
                        split_units(base + bodies - 1)
                    if half == 0:
                        split_tiles(src, 0, tiles + (bodies - 1) * RING)
                dve.wait_ge(unit_used, (first_group + 2 * bodies) * RING + RING)
                add_residual(V, 1)

            split_tiles(mixT, 0, 0)
            contraction(mixT, G_OUT, OUT_BODIES, 0, V2)
            normalise(A2, V2)
            transposed_lo(A2, V2, PAR_GFFN)
            did(v.memset(fg[:, :, 0:FTAPS - 1], 0.0), V2, "fpad")
            after(dve, V2, "fpad")

            with dve.Fori(0, UP_ITERS) as j:
                g0 = j * 2 + G_UP
                n0 = j * 2 + (G_UP - NOT_BANKED)

                def fpar(n, k):
                    return par[:, bass.ds(j * (2 * FFN_PAR) + (PAR_FFN + n * FFN_PAR + k), 1)]

                split_units(g0 + 1)
                add_half(n0, 0, fg[:, :, FTAPS - 1:])
                dve.wait_ge(group_free, freed(n0))
                for k in range(FTAPS):
                    for n in range(2):
                        tap = fg[:, n, k:k + S]
                        if k == 0:
                            did(v.tensor_scalar(fc[:, n, :], tap, fpar(n, k), fpar(n, FTAPS), ALU.mult, ALU.add),
                                V3, f"c{n}_{k}")
                        else:
                            after(dve, V3, f"c{n}_{k - 1}", j)
                            did(v.scalar_tensor_tensor(out=fc[:, n, :], in0=tap, scalar=fpar(n, k), in1=fc[:, n, :],
                                                       op0=ALU.mult, op1=ALU.add), V3, f"c{n}_{k}")
                split_units(g0 + 2)
                add_half(n0 + 1, 1, fu[:])
                dve.wait_ge(group_free, freed(n0 + 1))
                after(dve, A3, "silu", j)
                did(v.tensor_tensor(act[:, bass.ds(j * 2, 2), :], fu[:], fs[:], ALU.mult), V3, "act")

            split_tiles(act, 0, 2 * KT)
            contraction(act, G_DOWN, DOWN_BODIES, 2 * KT, V4)
            dve.wait_ge(gfin_landed, 16)
            norm_scale(A4, V4)
            for r in range(ROWS):
                for c in range(2):
                    cols = slice(c * HALF, (c + 1) * HALF)
                    did(v.scalar_tensor_tensor(out=xn[:, r, cols], in0=xres[:, r, cols], scalar=small[:, 6 + r:7 + r],
                                               in1=gfin[:, cols], op0=ALU.mult, op1=ALU.mult), V4, f"y{r}_{c}")

        @block.gpsimd
        def _(pool):
            pool.dma_start(cst[:], const_in).then_inc(par_landed, 16)
            pool.dma_start(par[:], par_in).then_inc(par_landed, 16)
            pool.dma_start(gw, gate_w.rearrange("p (k n) -> p k n", k=KT)).then_inc(gate_landed, 16)
            after(pool, V0, "gw_lo")
            pool.dma_start(gfin[:], gfin_in.to_broadcast([P, D])).then_inc(gfin_landed, 16)
            pool.wait_ge(par_landed, 32)
            with pool.Fori(0, H) as i:
                after(pool, A1, "decay", i)
                for n, col in enumerate((0, S)):
                    did(nc.gpsimd.tensor_tensor(decay[:, col:col + P], decay[:, col:col + P], tri, ALU.mult), L1, f"mask{n}")

        @block.tensor
        def _(pe):
            mm = nc.tensor.matmul

            def transposes(V, E, first=False):
                for b in range(KT // 2):
                    for r in range(ROWS):
                        after(pe, V, f"xn{r}_{b // 2}")
                    if b >= 4:
                        after(pe, V, f"t{b - 4}")
                    for n in range(2):
                        for r in range(ROWS):
                            kt = 2 * b + n
                            ins = nc.tensor.transpose(ps[:, 4 + b % 4, n * S + r * P:n * S + (r + 1) * P],
                                                      xn[:, r, kt * P:(kt + 1) * P], ident)
                            if first and b == 0 and n == 0 and r == 0:
                                ins.then_inc(unit_used, RING)
                    did(ins, E, f"t{b}")

            def group(g, n_banked, pair, rows_out=False):
                pe.wait_ge(group_free, n_banked + 1)
                for s in range(RING):
                    pe.wait_ge(lo_ready, g * RING + (s + 1 + RING))
                    for c in range(CH):
                        kt = s * CH + c
                        for n in range(2):
                            full, rest = ps[:, 2 * pair + n, :], ps[:, 2 * pair + n, COLS:2 * COLS]
                            cut = slice(n * P, (n + 1) * P)
                            if rows_out:
                                mm(full, xT[:, kt, 0, cut], w[:, s, c, :, :].rearrange("p a n -> p (a n)"),
                                   start=kt == 0, stop=False)
                                ins = mm(rest, xT[:, kt, 1, cut], w[:, s, c, 0, :], start=False, stop=kt == KT - 1)
                            else:
                                mm(full, w[:, s, c, 0, cut], xT[:, kt, :, :].rearrange("p a n -> p (a n)"),
                                   start=kt == 0, stop=False)
                                ins = mm(rest, w[:, s, c, 1, cut], xT[:, kt, 0, :], start=False, stop=kt == KT - 1)
                    ins.then_inc(unit_used, 1)
                    yield s

            def whole_group(*args, **kw):
                for _ in group(*args, **kw):
                    pass

            pe.wait_ge(par_landed, 32)
            transposes(V0, E0, first=True)
            after(pe, V0, "gw_lo")
            for kt in range(KT):
                mm(ps[:, B_SC, :], gwh[:, kt, :], xT[:, kt, :, :].rearrange("p a n -> p (a n)"), start=kt == 0, stop=False)
                ins = mm(ps[:, B_SC, S:2 * S], gwl[:, kt, :], xT[:, kt, 0, :], start=False, stop=kt == KT - 1)
            did(ins, E0, "gates")
            after(pe, V0, "gdif")
            for r in range(ROWS):
                did(nc.tensor.transpose(ps[:, 5 + r, 0:H], gdif[:, r * P:(r + 1) * P], cst[0:H, C_ID:C_ID + H]), E0, f"gcol{r}")
            after(pe, V0, "gcol1")
            after(pe, V0, "neg2")
            for h in range(H):
                did(mm(ps[:, 4 + h, :], cst[0:H, C_SEL + h * P:C_SEL + (h + 1) * P], neg[:].rearrange("p a t -> p (a t)"),
                       start=True, stop=True), E0, f"bc{h}")

            with pe.Fori(0, H) as i:
                g0 = i * MIX_GROUPS + G_MIX
                whole_group(g0, g0, 0)
                whole_group(g0 + 1, g0 + 1, 1)
                whole_group(g0 + 2, g0 + 2, 0, rows_out=True)
                pe.wait_ge(group_free, freed(g0 + 1))
                pe.wait_ge(act_step, A1.after("i_tanh1", i - 1))
                for n in range(2):
                    mm(ps[:, B_SC, 0:S], kT[:, n, 0:P], qT[:, n, :], start=n == 0, stop=n == 1)
                for n in range(2):
                    ins = mm(ps[:, B_SC, S:S + P], kT[:, n, P:S], qT[:, n, P:S], start=n == 0, stop=n == 1)
                did(ins, E1, "scores")
                whole_group(g0 + 3, g0 + 3, 1)
                after(pe, V1, "pT", i)
                pe.wait_ge(group_free, freed(g0 + 2))
                for n in range(2):
                    cut = slice(n * P, (n + 1) * P)
                    mm(ps[:, B_PV, n * S:(n + 1) * S], vN[:, 0, cut], pT[:, 0:S], start=True, stop=False)
                    mm(ps[:, B_PV, n * S + P:(n + 1) * S], vN[:, 1, cut], pT[:, S:S + P], start=False, stop=True)
                mm(ps[:, B_DEN, 0:S], ones, pT[:, 0:S], start=True, stop=False)
                did(mm(ps[:, B_DEN, P:S], ones, pT[:, S:S + P], start=False, stop=True), E1, "pv")
                whole_group(g0 + 4, g0 + 4, 0)
                after(pe, A1, "hsq", i)
                for n in range(2):
                    ins = mm(ps[:, B_DEN, S:2 * S], ones, hsq[:, n, :], start=n == 0, stop=n == 1)
                did(ins, E1, "rms")
                for s in group(g0 + 5, g0 + 5, 1):
                    if s == 2:
                        after(pe, V1, f"conv1_{TAPS - 1}", i)
                        pe.wait_ge(lru_w_landed, i * 32 + 32)
                        for bank, k in ((B_R, 0), (B_I, 1)):
                            for n in range(2):
                                ins = mm(ps[:, bank, n * S:(n + 1) * S], lru_w[:, n, k, :], xc[:, n, :], start=True, stop=True)
                        did(ins, E1, "lru")

            def contraction(first_group, bodies, count, banked_before):
                for half in range(2):
                    bank0 = 4 * (1 - half)
                    if half == 1:
                        pe.wait_ge(group_free, banked_before + FREE_AT_START)

                    def body(b, first=False, last=False):
                        for s in range(RING):
                            unit = b * RING + s
                            pe.wait_ge(lo_ready, unit + ((first_group + half * bodies) * RING + 1 + RING))
                            pe.wait_ge(a_lo_ready, unit + (count + half * bodies * RING + 1))
                            for r in range(ROWS):
                                cut = slice(r * P, (r + 1) * P)
                                for a_part, w_part in ((0, 0), (0, 1), (1, 0)):
                                    for n in range(2):
                                        ins = mm(ps[:, bank0 + 2 * r + n, :], aT[:, s, a_part, cut],
                                                 w[:, s, 2 * n:2 * n + 2, w_part, :],
                                                 start=first and s == 0 and a_part == 0 and w_part == 0,
                                                 stop=last and s == RING - 1 and a_part == 1)
                            ins.then_inc(unit_used, 1)

                    body(0, first=True)
                    with pe.Fori(1, bodies - 1) as b:
                        body(b)
                    body(bodies - 1, last=True)

            after(pe, A1, "i_tanh1", H - 1)
            contraction(G_OUT, OUT_BODIES, 0, G_OUT)
            transposes(V2, E2)
            after(pe, V2, f"t{KT // 2 - 1}")
            with pe.Fori(0, UP_ITERS) as j:
                for g in range(2):
                    whole_group(j * 2 + (G_UP + g), j * 2 + (G_UP - NOT_BANKED + g), g)
            contraction(G_DOWN, DOWN_BODIES, 2 * KT, G_DOWN - NOT_BANKED)


_WEIGHTS = ["w_in", "w_out", "w_up", "w_down"]


def kernel(**inputs):
    import numpy as np
    import concourse.bacc as bacc
    from concourse.bass_utils import run_bass_kernel_spmd

    a = {k: np.asarray(v) for k, v in inputs.items()}

    def cols(v, n):
        return v.reshape(n, P).T

    lru = np.stack([cols(t, LBLK) for t in (*a["lru_conv_w"][0], a["lru_conv_b"][0], a["lru_ba"][0], a["lru_bx"][0],
                                            a["lru_lambda"][0])], axis=2)
    ffn = np.stack([cols(t, FT) for t in (*a["ffn_conv_w"][0], a["ffn_conv_b"][0])], axis=2)
    bias = np.zeros((P, 1), np.float32)
    bias[0:H, 0] = a["b_gate_m"][0, :H]
    bias[F_ROW:F_ROW + H, 0] = a["b_gate_m"][0, H:]
    par = np.concatenate([cols(a["norm_mix_g"][0], KT), cols(a["norm_ffn_g"][0], KT),
                          cols(a["mlstm_norm_g"][0].reshape(-1), 2 * H),
                          lru.reshape(P, -1), ffn.reshape(P, -1), bias], axis=1)
    gate = np.zeros((P, KT, P), np.float32)
    gate_cols = a["w_in"][0][:, 4 * D_M:4 * D_M + 2 * H].reshape(KT, P, 2 * H).transpose(1, 0, 2)
    gate[:, :, 0:H] = gate_cols[:, :, :H]
    gate[:, :, F_ROW:F_ROW + H] = gate_cols[:, :, H:]
    const = np.zeros((P, NCONST), np.float32)
    const[:, C_ID:C_ID + P] = np.eye(P)
    const[:, C_TRI:C_TRI + P] = np.triu(np.ones((P, P)))
    const[:, C_ONE:C_ONE + P] = 1.0
    for h in range(H):
        const[h, C_SEL + h * P:C_SEL + (h + 1) * P] = 1.0

    arrays = {"x": a["x"], **{n: a[n][0] for n in _WEIGHTS}, "wa": a["lru_wa"][0], "wx": a["lru_wx"][0],
              "gate_w": gate.reshape(P, -1), "par": par, "const": const, "gfin": a["norm_final_g"].reshape(1, D)}
    nc = bacc.Bacc("TRN2", target_bir_lowering=False, num_devices=1)
    in_map, args = {}, []
    for name, array in arrays.items():
        in_map[f"{name}_dram"] = np.ascontiguousarray(array)
        args.append(nc.dram_tensor(f"{name}_dram", array.shape, F32, kind="ExternalInput").ap())
    y = nc.dram_tensor("y_dram", (1, S, D), F32, kind="ExternalOutput").ap()
    hybrid_block(nc, *args, y)
    result = run_bass_kernel_spmd(nc, [in_map], core_ids=[0])
    return result.results[0]["y_dram"]
```

```python
from contextlib import ExitStack

import concourse.bass as bass
from concourse import mybir

F32 = mybir.dt.float32
F32R = mybir.dt.float32r
ALU = mybir.AluOpType
ACT = mybir.ActivationFunctionType

P = 128
D = 2048
S = 256
KT = D // P
ROWS = S // P
H = 4
DH = 256
D_M = H * DH
D_L = D - D_M
LBLK = D_L // P
TAPS = 4
D_FF = 5632
FT = D_FF // P
FTAPS = 3
EPS = 1e-6
LRU_C = 8.0

RING = 4
CH = 4
COLS = 256
HALF = CH * COLS
BANK = 512

MIX_GROUPS = 6
OUT_BODIES = KT // RING
UP_ITERS = D_FF // COLS
DOWN_BODIES = FT // RING
G_MIX = 0
G_OUT = G_MIX + H * MIX_GROUPS
G_UP = G_OUT + 2 * OUT_BODIES
G_DOWN = G_UP + 2 * UP_ITERS
G_END = G_DOWN + 2 * DOWN_BODIES

NOT_BANKED = 2 * OUT_BODIES
FREE_AT_START = 2

PAR_GMIX = 0
PAR_GFFN = PAR_GMIX + KT
PAR_HEAD = PAR_GFFN + KT
PAR_LRU = PAR_HEAD + 2 * H
LRU_PAR = 8
PAR_FFN = PAR_LRU + LBLK * LRU_PAR
FFN_PAR = 4
PAR_GATE = PAR_FFN + FT * FFN_PAR
NPAR = PAR_GATE + 1
F_ROW = 32

C_ID, C_TRI = 0, P
NCONST = 2 * P
SSQ, VAR, STD, C_EPS, RSTD, WARM, C_TINY = 0, 4, 6, 8, 10, 12, 13
TINY = 1e-34
FLOOR_LN = 47.0


class Steps:

    def __init__(self, sem, base, names):
        self.sem, self.base, self.names = sem, base, names.split()
        self.n = len(self.names)

    def after(self, name, i=0):
        return i * self.n + (self.base + self.names.index(name) + 1)

    def end(self, iterations=1):
        return self.base + self.n * iterations


def hybrid_block(nc, x, w_in, w_out, w_up, w_down, wa, wx, gate_w, par_in, const_in, sel_in, gfin_in, out):
    with ExitStack() as ctx:
        def sem(name):
            return ctx.enter_context(nc.semaphore(name))

        def sb(name, shape, dt=F32, where=ctx):
            return where.enter_context(nc.sbuf_tensor(name, shape, dt))

        xres = sb("xres", [P, ROWS, D])
        xn = sb("xn", [P, ROWS, D])
        xT = sb("xT", [P, KT, 2, S], F32R)
        raw = sb("raw", [P, RING, HALF])
        w = sb("w", [P, RING, CH, 2, COLS], F32R)
        aT = sb("aT", [P, RING, 2, S], F32R)
        par = sb("par", [P, NPAR])
        cst = sb("cst", [P, NCONST])
        gfin = sb("gfin", [P, D])
        small = sb("small", [P, 16])
        ones = sb("ones", [P, P])
        sel = sb("sel", [H, H, P])
        ident = cst[:, C_ID:C_ID + P]
        tri = cst[:, C_TRI:C_TRI + P]

        gw = gfin[:].rearrange("p (k n) -> p k n", k=KT)
        gate_cols = ExitStack()
        gwh = sb("gwh", [P, KT, P], F32R, where=gate_cols)
        gwl = sb("gwl", [P, KT, P], F32R, where=gate_cols)
        gate_cols.close()
        mixer = ExitStack()
        mixT = sb("mixT", [P, KT, S], where=mixer)
        qT = sb("qT", [P, 2, S], where=mixer)
        kT = sb("kT", [P, 2, S], where=mixer)
        vN = sb("vN", [P, ROWS, DH], where=mixer)
        negM = sb("negM", [P, H, S], where=mixer)
        floor = sb("floor", [P, H, S], where=mixer)
        gcol = sb("gcol", [P, ROWS, H], where=mixer)
        decay = sb("decay", [P, 3 * P], where=mixer)
        pT = sb("pT", [P, 3 * P], where=mixer)
        den = sb("den", [P, S], where=mixer)
        hT = sb("hT", [P, 2, S], where=mixer)
        hsq = sb("hsq", [P, 2, S], where=mixer)
        oT = sb("oT", [P, 2, S], where=mixer)
        rstd_h = sb("rstd_h", [P, S], where=mixer)
        xr = sb("xr", [P, 2, S + TAPS - 1], where=mixer)
        xc = sb("xc", [P, 2, S], where=mixer)
        rg = sb("rg", [P, 2, S], where=mixer)
        ig = sb("ig", [P, 2, S], where=mixer)
        lruA = sb("lruA", [P, 2, S], where=mixer)
        lruT = sb("lruT", [P, 2, S], where=mixer)
        lruU = sb("lruU", [P, 2, S], where=mixer)
        lruH = sb("lruH", [P, 2, S], where=mixer)
        gr = sb("gr", [P, 2, S], where=mixer)
        gr2 = sb("gr2", [P, 2, S], where=mixer)
        lru_w = sb("lru_w", [P, 2, 2, P], where=mixer)
        lp = sb("lp", [P, 4, LBLK], where=mixer)
        hg = sb("hg", [P, 2 * H], where=mixer)
        gates = ExitStack()
        grow = sb("grow", [64, S], where=gates)
        gtmp = sb("gtmp", [64, S], where=gates)
        logf = sb("logf", [H, S], where=gates)
        fsum = sb("fsum", [H, S], where=gates)
        gdif = sb("gdif", [H, S], where=gates)
        neg = sb("neg", [H, 2, S], where=gates)
        gates.close()
        mixer.close()
        ffn = ExitStack()
        act = sb("act", [P, FT, S], where=ffn)
        fg = sb("fg", [P, 2, S + FTAPS - 1], where=ffn)
        fc = sb("fc", [P, 2, S], where=ffn)
        fs = sb("fs", [P, 2, S], where=ffn)
        fu = sb("fu", [P, 2, S], where=ffn)
        ffn.close()

        ps = ctx.enter_context(nc.psum_tensor("ps", [P, 8, BANK], F32))
        B_SC, B_R, B_PV, B_DEN = 4, 5, 6, 7
        B_I = B_SC

        x_landed = [sem(f"x_landed{n}") for n in range(2 * ROWS)]
        par_landed = sem("par_landed")
        gate_landed = sem("gate_landed")
        gfin_landed = sem("gfin_landed")
        lru_w_landed = sem("lru_w_landed")
        raw_landed = [sem(f"raw_landed{s}") for s in range(RING)]
        hi_ready = sem("hi_ready")
        lo_ready = sem("lo_ready")
        unit_used = sem("unit_used")
        group_free = sem("group_free")
        half_copied = sem("half_copied")
        a_hi_ready = sem("a_hi_ready")
        a_lo_ready = sem("a_lo_ready")
        stored = sem("stored")
        act_step, dve_step, pe_step, pool_step = sem("act_step"), sem("dve_step"), sem("pe_step"), sem("pool_step")

        stats_act = "warm sq0_0 sq0_1 sq1_0 sq1_1 std "
        stats_dve = "ssum var rstd "
        xn_steps = " ".join(f"xn{r}_{c}" for c in range(4) for r in range(ROWS)) + " "
        tr_steps = " ".join(f"t{b}" for b in range(KT // 2)) + " "
        out_steps = "out0_0 out0_1 out1_0 out1_1 "
        A0 = Steps(act_step, 0, stats_act + tr_steps + "gw_hi lam_exp lam_ln gate_half f_exp f_ln floor0 floor1 floor2 floor3")
        V0 = Steps(dve_step, 0, "start " + stats_dve + xn_steps + tr_steps + "gw_lo lam_neg lam_abs lam_relu softplus c_col"
                   " half_bias nc_col hg gate_sum gate_bias f_neg f_abs logf fsum gdif cmax neg_M neg_m neg_clip gcol0 gcol1"
                   " negM0 negM1 negM2 negM3 pads")
        E0 = Steps(pe_step, 0, tr_steps + "gates gcol0 gcol1 bc0 bc1 bc2 bc3")
        A1 = Steps(act_step, A0.end(), "decay hsq rms_std o_tanh r_tanh0 r_tanh1 i_tanh0 i_tanh1 lru_a0 lru_a1 lru_t0 lru_t1 lru_s g_tanh")
        V1 = Steps(dve_step, V0.end(), "arg0 arg1 pT dneg den dsq hvar"
                   " conv0_0 conv1_0 conv0_1 conv1_1 conv0_2 conv1_2 conv0_3 conv1_3 rstd og mix0 mix1"
                   " ux asq w u scan0 scan1 gsq gp gq gh mixl")
        E1 = Steps(pe_step, E0.end(), "scores pv rms lru")
        L1 = Steps(pool_step, 0, "mask0 mask1")
        A2 = Steps(act_step, A1.end(H), stats_act + tr_steps)
        V2 = Steps(dve_step, V1.end(H), out_steps + stats_dve + xn_steps + tr_steps + "fpad")
        E2 = Steps(pe_step, E1.end(H), tr_steps)
        A3 = Steps(act_step, A2.end(), "silu")
        V3 = Steps(dve_step, V2.end(), "c0_0 c1_0 c0_1 c1_1 c0_2 c1_2 act")
        A4 = Steps(act_step, A3.end(UP_ITERS), stats_act + "y0 y1")
        V4 = Steps(dve_step, V3.end(UP_ITERS), out_steps + stats_dve + "y0 y1")
        L4 = Steps(pool_step, L1.end(H), "xg0 xg1")

        def freed(n):
            return n + (1 + FREE_AT_START)

        def after(eng, steps, name, i=0):
            eng.wait_ge(steps.sem, steps.after(name, i))

        def did(ins, steps, name, seen={}):
            key = id(steps)
            assert steps.names[seen.get(key, 0) % steps.n] == name, (name, steps.names[seen.get(key, 0) % steps.n])
            seen[key] = seen.get(key, 0) + 1
            ins.then_inc(steps.sem, 1)

        block = ctx.enter_context(nc.Block())

        @block.sync
        def _(sp):
            xv = x.rearrange("a (r p) (c d) -> (a r) c p d", p=P, c=2)
            for c in range(2):
                for r in range(ROWS):
                    sp.dma_start(xres[:, r, c * HALF:(c + 1) * HALF], xv[r, c]).then_inc(x_landed[c * ROWS + r], 16)

            def load(group, s, src, dst):
                sp.wait_ge(lo_ready, group * RING + s + 1)
                sp.dma_start(dst, src).then_inc(raw_landed[s], 16)

            in_v = w_in.rearrange("(s c p) n -> s p c n", c=CH, p=P)
            up_v = w_up.rearrange("(s c p) n -> s p c n", c=CH, p=P)

            def load_group(group, view, col):
                for s in range(RING):
                    load(group, s, view[s, :, :, bass.ds(col, COLS)],
                         raw[:, s, :].rearrange("p (c n) -> p c n", c=CH))

            def load_body(group, weights, b, half):
                rows = weights.rearrange("(b s p) n -> s p b n", s=RING, p=P)
                for s in range(RING):
                    load(group, s, rows[s, :, bass.ds(b, 1), half * HALF:(half + 1) * HALF],
                         raw[:, s, :].rearrange("p (b n) -> p b n", b=1))

            COL_Q, COL_K, COL_V, COL_O, COL_XR, COL_GR = 0, D_M, 2 * D_M, 3 * D_M, 4 * D_M + 2 * H, 4 * D_M + 2 * H + D_L
            wa_v = wa.rearrange("(i b) k j -> i k b j", b=2)
            wx_v = wx.rearrange("(i b) k j -> i k b j", b=2)

            def load_head(i, last):
                g0 = i * MIX_GROUPS + 2
                for g, col in enumerate((COL_V, COL_O, COL_XR, COL_GR)):
                    load_group(g0 + g, in_v, i * COLS + col)
                    if g == 1:
                        sp.wait_ge(pe_step, E1.after("lru", i - 1))
                        for n, view in enumerate((wa_v, wx_v)):
                            sp.dma_start(lru_w[:, :, n, :], view[bass.ds(i, 1)].rearrange("i k b j -> k (i b) j")).then_inc(lru_w_landed, 16)
                if not last:
                    load_group(g0 + 4, in_v, i * COLS + (COL_Q + COLS))
                    load_group(g0 + 5, in_v, i * COLS + (COL_K + COLS))

            load_group(0, in_v, COL_Q)
            load_group(1, in_v, COL_K)
            with sp.Fori(0, H - 1) as i:
                load_head(i, False)
            load_head(H - 1, True)
            for half in range(2):
                with sp.Fori(0, OUT_BODIES) as b:
                    load_body(b + (G_OUT + half * OUT_BODIES), w_out, b, half)
            with sp.Fori(0, UP_ITERS) as j:
                for g in range(2):
                    load_group(j * 2 + (G_UP + g), up_v, j * COLS + g * D_FF)
            for half in range(2):
                with sp.Fori(0, DOWN_BODIES) as b:
                    load_body(b + (G_DOWN + half * DOWN_BODIES), w_down, b, half)
            yv = out.rearrange("a (r p) (c d) -> (a r) c p d", p=P, c=2)
            for c, steps in ((0, A4), (1, V4)):
                for r in range(ROWS):
                    after(sp, steps, f"y{r}")
                    sp.dma_start(yv[r, c], xn[:, r, c * HALF:(c + 1) * HALF]).then_inc(stored, 16)
            sp.wait_ge(stored, 16 * ROWS * 2)

        @block.scalar
        def _(act_e):
            sc = nc.scalar

            def act_fn(out_, in_, fn=ACT.Copy, **kw):
                return sc.activation(out_, in_, fn, **kw)

            def round_units(group, slots=range(RING)):
                for s in slots:
                    act_e.wait_ge(raw_landed[s], group * 16 + 16)
                    act_e.wait_ge(unit_used, group * RING + s + 1)
                    act_fn(w[:, s, :, 0, :], raw[:, s, :].rearrange("p (c n) -> p c n", c=CH)).then_inc(hi_ready, 1)

            def round_tiles(src, first, slots=range(RING)):
                for s in slots:
                    act_fn(aT[:, s, 0, :], src[:, bass.ds(first + s, 1), :].rearrange("p a n -> p (a n)")).then_inc(a_hi_ready, 1)

            def copy_half(group, pair, dst):
                act_e.wait_ge(unit_used, group * RING + 2 * RING)
                act_fn(dst, ps[:, 2 * pair:2 * pair + 2, 0:COLS]).then_inc(half_copied, 1)

            def squares(A, half, landed):
                for r in range(ROWS):
                    landed(r)
                    cols = slice(half * HALF, (half + 1) * HALF)
                    n = SSQ + half * ROWS + r
                    did(act_fn(xn[:, r, cols], xres[:, r, cols], ACT.Square, accum_out=small[:, n:n + 1]), A, f"sq{half}_{r}")

            def warm_sqrt(A):
                did(act_fn(small[:, WARM:WARM + 1], small[:, C_EPS:C_EPS + 1], ACT.Sqrt), A, "warm")

            def std(A, V):
                after(act_e, V, "var")
                did(act_fn(small[:, STD:STD + ROWS], small[:, VAR:VAR + ROWS], ACT.Sqrt), A, "std")

            def transposed_hi(A, E, gains, b):
                after(act_e, E, f"t{b}")
                for n in range(2):
                    kt = 2 * b + n
                    ins = act_fn(xT[:, kt, 0, :], ps[:, 4 + b % 4, n * S:(n + 1) * S],
                                 scale=par[:, gains + kt:gains + kt + 1])
                did(ins, A, f"t{b}")

            after(act_e, V0, "start")
            warm_sqrt(A0)
            for half in range(2):
                squares(A0, half, lambda r: act_e.wait_ge(x_landed[half * ROWS + r], 16))
            std(A0, V0)
            act_e.wait_ge(par_landed, 48)
            for s in range(RING):
                transposed_hi(A0, E0, PAR_GMIX, 2 * s)
                transposed_hi(A0, E0, PAR_GMIX, 2 * s + 1)
                round_units(0, [s])
            act_e.wait_ge(gate_landed, 16)
            did(act_fn(gwh[:], gw), A0, "gw_hi")
            after(act_e, V0, "lam_abs")
            did(act_fn(lp[:, 2, :], lp[:, 2, :], ACT.Exp), A0, "lam_exp")
            after(act_e, A0, "lam_exp")
            did(act_fn(lp[:, 2, :], lp[:, 2, :], ACT.Ln, bias=1.0), A0, "lam_ln")
            round_units(1)
            copy_half(0, 0, qT[:])
            after(act_e, E0, "gates")
            did(act_fn(grow[:], ps[0:64, B_SC, 0:S]), A0, "gate_half")
            after(act_e, V0, "f_abs")
            did(act_fn(gtmp[F_ROW:F_ROW + H], gtmp[F_ROW:F_ROW + H], ACT.Exp), A0, "f_exp")
            after(act_e, A0, "f_exp")
            did(act_fn(gtmp[F_ROW:F_ROW + H], gtmp[F_ROW:F_ROW + H], ACT.Ln, bias=1.0), A0, "f_ln")
            round_units(2)
            copy_half(1, 1, kT[:])
            for h in range(H):
                after(act_e, E0, f"bc{h}")
                did(act_fn(floor[:, h, :], ps[:, 4 + h, S:2 * S], ACT.Exp), A0, f"floor{h}")

            def head(i, last):
                g0 = i * MIX_GROUPS + 2
                after(act_e, V1, "arg1", i)
                did(act_fn(decay[:], decay[:], ACT.Exp), A1, "decay")
                round_units(g0 + 1)
                copy_half(g0, 0, vN[:])
                round_units(g0 + 2)
                copy_half(g0 + 1, 1, oT[:])
                after(act_e, E1, "pv", i)
                did(act_fn(hsq[:].rearrange("p a t -> p (a t)"), ps[:, B_PV, :], ACT.Square), A1, "hsq")
                round_units(g0 + 3)
                copy_half(g0 + 2, 0, xr[:, :, TAPS - 1:])
                after(act_e, V1, "hvar", i)
                did(act_fn(rstd_h[:], rstd_h[:], ACT.Sqrt, bias=small[:, C_TINY:C_TINY + 1]), A1, "rms_std")
                act_e.wait_ge(group_free, freed(g0 + 1))
                did(act_fn(oT[:], oT[:], ACT.Tanh, scale=0.5), A1, "o_tanh")
                round_units(g0 + 4, range(3))
                after(act_e, E1, "lru", i)
                for n in range(2):
                    did(act_fn(rg[:, n, :], ps[:, B_R, n * S:(n + 1) * S], ACT.Tanh, scale=0.5,
                               bias=lp[:, 0, bass.ds(i * 2 + n, 1)]), A1, f"r_tanh{n}")
                for n in range(2):
                    did(act_fn(ig[:, n, :], ps[:, B_I, n * S:(n + 1) * S], ACT.Tanh, scale=0.5,
                               bias=lp[:, 1, bass.ds(i * 2 + n, 1)]), A1, f"i_tanh{n}")
                after(act_e, A1, "r_tanh1", i)
                for n in range(2):
                    did(act_fn(lruA[:, n, :], rg[:, n, :], ACT.Exp, scale=lp[:, 2, bass.ds(i * 2 + n, 1)],
                               bias=lp[:, 2, bass.ds(i * 2 + n, 1)]), A1, f"lru_a{n}")
                for n in range(2):
                    did(act_fn(lruT[:, n, :], rg[:, n, :], ACT.Tanh, scale=lp[:, 3, bass.ds(i * 2 + n, 1)],
                               bias=lp[:, 3, bass.ds(i * 2 + n, 1)]), A1, f"lru_t{n}")
                round_units(g0 + 4, range(3, RING))
                if last:
                    round_tiles(mixT, 0)
                after(act_e, V1, "w", i)
                did(act_fn(lruT[:], lruT[:], ACT.Sqrt, scale=0.25), A1, "lru_s")
                copy_half(g0 + 3, 1, gr[:])
                if not last:
                    round_units(g0 + 5)
                after(act_e, V1, "gq", i)
                did(act_fn(gr2[:], gr2[:], ACT.Tanh, scale=0.7978845608028654), A1, "g_tanh")
                if not last:
                    copy_half(g0 + 4, 0, qT[:])
                    round_units(g0 + 6)
                    copy_half(g0 + 5, 1, kT[:])

            with act_e.Fori(0, H - 1) as i:
                head(i, False)
            head(H - 1, True)

            def contraction(src, first_group, bodies, A, V):
                for half in range(2):
                    base = first_group + half * bodies + 1
                    if half == 1:
                        for s in range(RING):
                            round_units(base, [s])
                            round_tiles(src, RING, [s])
                        warm_sqrt(A)
                        squares(A, 0, lambda r: after(act_e, V, f"out0_{r}"))
                    with act_e.Fori(half, bodies - 1) as b:
                        for s in range(RING):
                            round_units(b + base, [s])
                            round_tiles(src, b * RING + RING, [s])
                    for s in range(RING):
                        if base + bodies - 1 < G_END:
                            round_units(base + bodies - 1, [s])
                        if half == 0:
                            round_tiles(src, 0, [s])

            after(act_e, V1, "mixl", H - 1)
            contraction(mixT, G_OUT, OUT_BODIES, A2, V2)
            squares(A2, 1, lambda r: after(act_e, V2, f"out1_{r}"))
            std(A2, V2)
            for b in range(KT // 2):
                transposed_hi(A2, E2, PAR_GFFN, b)

            def gate_post(group, j):
                copy_half(group, 0, fg[:, :, FTAPS - 1:])
                after(act_e, V3, "c1_2", j)
                did(act_fn(fs[:], fc[:], ACT.Silu), A3, "silu")

            round_units(G_UP + 1)
            gate_post(G_UP, 0)
            with act_e.Fori(0, UP_ITERS - 1) as j:
                round_units(j * 2 + (G_UP + 2))
                act_e.wait_ge(dve_step, V3.after("act", j - 1))
                copy_half(j * 2 + (G_UP + 1), 1, fu[:])
                round_units(j * 2 + (G_UP + 3))
                gate_post(j * 2 + (G_UP + 2), j + 1)
            for s in range(RING):
                round_units(G_DOWN, [s])
                round_tiles(act, 0, [s])
            copy_half(G_DOWN - 1, 1, fu[:])
            after(act_e, V3, "act", UP_ITERS - 1)
            contraction(act, G_DOWN, DOWN_BODIES, A4, V4)
            squares(A4, 1, lambda r: after(act_e, V4, f"out1_{r}"))
            std(A4, V4)
            after(act_e, V4, "rstd")
            for r in range(ROWS):
                after(act_e, L4, f"xg{r}")
                did(act_fn(xn[:, r, 0:HALF], xn[:, r, 0:HALF], scale=small[:, RSTD + r:RSTD + r + 1]), A4, f"y{r}")

        @block.vector
        def _(dve):
            v = nc.vector

            def split_units(group, slots=range(RING)):
                for s in slots:
                    dve.wait_ge(hi_ready, group * RING + s + 1)
                    v.tensor_tensor(w[:, s, :, 1, :], raw[:, s, :].rearrange("p (c n) -> p c n", c=CH),
                                    w[:, s, :, 0, :], ALU.subtract).then_inc(lo_ready, 1)

            def split_tiles(src, first, count, slots=range(RING)):
                for s in slots:
                    dve.wait_ge(a_hi_ready, count + s + 1)
                    v.tensor_tensor(aT[:, s, 1, :], src[:, bass.ds(first + s, 1), :].rearrange("p a n -> p (a n)"),
                                    aT[:, s, 0, :], ALU.subtract).then_inc(a_lo_ready, 1)

            def add_half(n, pair, dst):
                dve.wait_ge(half_copied, n + 1)
                v.tensor_tensor(dst, ps[:, 2 * pair:2 * pair + 2, COLS:2 * COLS], dst, ALU.add).then_inc(group_free, 1)

            def norm_scale(A, V):
                after(dve, A, "sq1_1")
                did(v.tensor_tensor(small[:, VAR:VAR + ROWS], small[:, SSQ:SSQ + ROWS], small[:, SSQ + ROWS:SSQ + 2 * ROWS], ALU.add),
                    V, "ssum")
                after(dve, V, "ssum")
                did(v.tensor_scalar(small[:, VAR:VAR + ROWS], small[:, VAR:VAR + ROWS], 1.0 / D, EPS, ALU.mult, ALU.add), V, "var")
                after(dve, A, "std")
                did(v.reciprocal(small[:, RSTD:RSTD + ROWS], small[:, STD:STD + ROWS]), V, "rstd")
                after(dve, V, "rstd")

            def normalise(A, V):
                norm_scale(A, V)
                for c in range(4):
                    for r in range(ROWS):
                        cols = slice(c * BANK, (c + 1) * BANK)
                        did(v.tensor_scalar(xn[:, r, cols], xres[:, r, cols], small[:, RSTD + r:RSTD + r + 1], None, ALU.mult),
                            V, f"xn{r}_{c}")

            def transposed_lo(A, V, gains, b):
                after(dve, A, f"t{b}")
                for n in range(2):
                    kt = 2 * b + n
                    ins = v.scalar_tensor_tensor(out=xT[:, kt, 1, :], in0=ps[:, 4 + b % 4, n * S:(n + 1) * S],
                                                 scalar=par[:, gains + kt:gains + kt + 1], in1=xT[:, kt, 0, :],
                                                 op0=ALU.mult, op1=ALU.subtract)
                did(ins, V, f"t{b}")

            v.memset(small[:], 0.0).then_inc(lo_ready, RING)
            dve.wait_ge(lo_ready, RING)
            v.memset(small[:, C_EPS + 1:C_EPS + 2], 0.0).then_inc(group_free, FREE_AT_START)
            v.memset(ones[:], 1.0)
            v.memset(small[:, C_TINY:C_TINY + 1], TINY)
            did(v.memset(small[:, C_EPS:C_EPS + 1], EPS), V0, "start")
            normalise(A0, V0)
            dve.wait_ge(par_landed, 48)
            for s in range(RING):
                transposed_lo(A0, V0, PAR_GMIX, 2 * s)
                transposed_lo(A0, V0, PAR_GMIX, 2 * s + 1)
                split_units(0, [s])
            after(dve, A0, "gw_hi")
            did(v.tensor_tensor(gwl[:], gw, gwh[:], ALU.subtract), V0, "gw_lo")

            lru_par = par[:, PAR_LRU:PAR_LRU + LBLK * LRU_PAR].rearrange("p (b n) -> p n b", n=LRU_PAR)
            lam = lru_par[:, 7, :]
            did(v.tensor_scalar(lp[:, 3, :], lam, -1.0, None, ALU.mult), V0, "lam_neg")
            after(dve, V0, "lam_neg")
            did(v.tensor_tensor(lp[:, 2, :], lp[:, 3, :], lam, ALU.min), V0, "lam_abs")
            after(dve, V0, "lam_abs")
            did(v.tensor_scalar(lp[:, 3, :], lp[:, 3, :], 0.0, None, ALU.max), V0, "lam_relu")
            after(dve, A0, "lam_ln")
            after(dve, V0, "lam_relu")
            did(v.tensor_tensor(lp[:, 3, :], lp[:, 3, :], lp[:, 2, :], ALU.add), V0, "softplus")
            after(dve, V0, "softplus")
            did(v.tensor_scalar(lp[:, 2, :], lp[:, 3, :], -LRU_C / 2, None, ALU.mult), V0, "c_col")
            did(v.tensor_scalar(lp[:, 0:2, :], lru_par[:, 5:7, :], 0.5, None, ALU.mult), V0, "half_bias")
            after(dve, V0, "half_bias")
            did(v.tensor_scalar(lp[:, 3, :], lp[:, 3, :], LRU_C / 2, None, ALU.mult), V0, "nc_col")
            did(v.tensor_scalar(hg[:], par[:, PAR_HEAD:PAR_HEAD + 2 * H], 0.5, None, ALU.mult), V0, "hg")

            split_units(1)
            add_half(0, 0, qT[:])
            frow = slice(F_ROW, F_ROW + H)
            after(dve, A0, "gate_half")
            did(v.tensor_tensor(grow[:], ps[0:64, B_SC, S:2 * S], grow[:], ALU.add), V0, "gate_sum")
            after(dve, V0, "gate_sum")
            did(v.tensor_scalar(grow[:], grow[:], par[0:64, PAR_GATE:PAR_GATE + 1], None, ALU.add), V0, "gate_bias")
            after(dve, V0, "gate_bias")
            did(v.tensor_scalar(gtmp[frow], grow[frow], -1.0, None, ALU.mult), V0, "f_neg")
            after(dve, V0, "f_neg")
            did(v.tensor_tensor(gtmp[frow], gtmp[frow], grow[frow], ALU.min), V0, "f_abs")
            after(dve, A0, "f_ln")
            did(v.scalar_tensor_tensor(out=logf[:], in0=grow[frow], scalar=0.0, in1=gtmp[frow],
                                       op0=ALU.min, op1=ALU.subtract), V0, "logf")
            after(dve, V0, "logf")
            one_row = ones[0:H, 0:1].to_broadcast([H, S])
            did(v.tensor_tensor_scan(fsum[:], one_row, logf[:], 0.0, ALU.mult, ALU.add), V0, "fsum")
            after(dve, V0, "fsum")
            did(v.tensor_tensor(gdif[:], grow[0:H], fsum[:], ALU.subtract), V0, "gdif")
            after(dve, V0, "gdif")
            did(v.tensor_tensor_scan(logf[:], one_row, gdif[:], 0.0, ALU.mult, ALU.max), V0, "cmax")
            after(dve, V0, "cmax")
            did(v.tensor_scalar(neg[:, 0, :], logf[:], -1.0, None, ALU.mult), V0, "neg_M")
            after(dve, V0, "neg_M")
            did(v.tensor_tensor(neg[:, 1, :], neg[:, 0, :], fsum[:], ALU.subtract), V0, "neg_m")
            after(dve, V0, "neg_m")
            did(v.tensor_scalar(neg[:, 1, :], neg[:, 1, :], FLOOR_LN, None, ALU.min), V0, "neg_clip")
            split_units(2)
            add_half(1, 1, kT[:])
            for r in range(ROWS):
                after(dve, E0, f"gcol{r}")
                did(v.tensor_copy(gcol[:, r, :], ps[:, 5 + r, 0:H]), V0, f"gcol{r}")
            for h in range(H):
                after(dve, A0, f"floor{h}")
                did(v.tensor_copy(negM[:, h, :], ps[:, 4 + h, 0:S]), V0, f"negM{h}")
            did(v.memset(xr[:, :, 0:TAPS - 1], 0.0), V0, "pads")
            after(dve, V0, "pads")

            def head(i, last):
                g0 = i * MIX_GROUPS + 2

                def lpar(n, k):
                    return par[:, bass.ds(i * (2 * LRU_PAR) + (PAR_LRU + n * LRU_PAR + k), 1)]

                def chain(name):
                    after(dve, V1, name, i)

                minus_m = negM[:, bass.ds(i, 1), :].rearrange("p a t -> p (a t)")
                did(v.tensor_scalar(decay[:, 0:S], minus_m, gcol[:, 0, bass.ds(i, 1)], 0.0, ALU.add, ALU.min), V1, "arg0")
                did(v.tensor_scalar(decay[:, S:S + P], negM[:, bass.ds(i, 1), P:S].rearrange("p a t -> p (a t)"),
                                    gcol[:, 1, bass.ds(i, 1)], 0.0, ALU.add, ALU.min), V1, "arg1")
                split_units(g0 + 1)
                add_half(g0, 0, vN[:])
                after(dve, L1, "mask1", i)
                after(dve, E1, "scores", i)
                did(v.scalar_tensor_tensor(out=pT[:], in0=ps[:, B_SC, 0:3 * P], scalar=DH ** -0.5, in1=decay[:],
                                           op0=ALU.mult, op1=ALU.mult), V1, "pT")
                split_units(g0 + 2)
                add_half(g0 + 1, 1, oT[:])
                after(dve, E1, "pv", i)
                did(v.scalar_tensor_tensor(out=den[:], in0=ps[:, B_DEN, 0:S], scalar=-1.0,
                                           in1=floor[:, bass.ds(i, 1), :].rearrange("p a t -> p (a t)"),
                                           op0=ALU.mult, op1=ALU.max), V1, "dneg")
                chain("dneg")
                did(v.tensor_tensor(den[:], ps[:, B_DEN, 0:S], den[:], ALU.max), V1, "den")
                chain("den")
                did(v.scalar_tensor_tensor(out=den[:], in0=den[:], scalar=EPS, in1=den[:], op0=ALU.mult, op1=ALU.mult), V1, "dsq")
                split_units(g0 + 3)
                add_half(g0 + 2, 0, xr[:, :, TAPS - 1:])
                after(dve, E1, "rms", i)
                chain("dsq")
                did(v.scalar_tensor_tensor(out=rstd_h[:], in0=ps[:, B_DEN, S:2 * S], scalar=1.0 / DH, in1=den[:],
                                           op0=ALU.mult, op1=ALU.add), V1, "hvar")
                dve.wait_ge(group_free, freed(g0 + 2))
                for k in range(TAPS):
                    for n in range(2):
                        tap = xr[:, n, k:k + S]
                        if k == 0:
                            did(v.tensor_scalar(xc[:, n, :], tap, lpar(n, k), lpar(n, TAPS), ALU.mult, ALU.add),
                                V1, f"conv{n}_{k}")
                        else:
                            chain(f"conv{n}_{k - 1}")
                            did(v.scalar_tensor_tensor(out=xc[:, n, :], in0=tap, scalar=lpar(n, k), in1=xc[:, n, :],
                                                       op0=ALU.mult, op1=ALU.add), V1, f"conv{n}_{k}")
                after(dve, A1, "rms_std", i)
                did(v.reciprocal(rstd_h[:], rstd_h[:]), V1, "rstd")
                after(dve, A1, "o_tanh", i)
                did(v.scalar_tensor_tensor(out=hT[:].rearrange("p a t -> p (a t)"), in0=oT[:].rearrange("p a t -> p (a t)"),
                                           scalar=1.0, in1=ps[:, B_PV, :], op0=ALU.add, op1=ALU.mult), V1, "og")
                chain("og")
                for n in range(2):
                    did(v.scalar_tensor_tensor(out=mixT[:, bass.ds(i * 2 + n, 1), :].rearrange("p a t -> p (a t)"),
                                               in0=hT[:, n, :], scalar=hg[:, bass.ds(i * 2 + n, 1)], in1=rstd_h[:],
                                               op0=ALU.mult, op1=ALU.mult), V1, f"mix{n}")
                split_units(g0 + 4, range(3))
                after(dve, A1, "i_tanh1", i)
                did(v.scalar_tensor_tensor(out=lruU[:], in0=ig[:], scalar=1.0, in1=xc[:], op0=ALU.add, op1=ALU.mult), V1, "ux")
                after(dve, A1, "lru_a1", i)
                did(v.tensor_tensor(lruH[:], lruA[:], lruA[:], ALU.mult), V1, "asq")
                after(dve, A1, "lru_t1", i)
                chain("asq")
                did(v.scalar_tensor_tensor(out=lruT[:], in0=lruH[:], scalar=1.0, in1=lruT[:], op0=ALU.add, op1=ALU.mult), V1, "w")
                split_units(g0 + 4, range(3, RING))
                if last:
                    split_tiles(mixT, 0, 0)
                after(dve, A1, "lru_s", i)
                did(v.tensor_tensor(lruU[:], lruU[:], lruT[:], ALU.mult), V1, "u")
                chain("u")
                for n in range(2):
                    did(v.tensor_tensor_scan(lruH[:, n, :], lruA[:, n, :], lruU[:, n, :], 0.0, ALU.mult, ALU.add),
                        V1, f"scan{n}")
                add_half(g0 + 3, 1, gr[:])
                dve.wait_ge(group_free, freed(g0 + 3))
                did(v.tensor_tensor(gr2[:], gr[:], gr[:], ALU.mult), V1, "gsq")
                chain("gsq")
                did(v.tensor_scalar(gr2[:], gr2[:], 0.044715, 1.0, ALU.mult, ALU.add), V1, "gp")
                chain("gp")
                did(v.tensor_tensor(gr2[:], gr2[:], gr[:], ALU.mult), V1, "gq")
                if not last:
                    split_units(g0 + 5)
                after(dve, A1, "g_tanh", i)
                did(v.scalar_tensor_tensor(out=gr2[:], in0=gr2[:], scalar=1.0, in1=gr[:], op0=ALU.add, op1=ALU.mult), V1, "gh")
                chain("gh")
                did(v.scalar_tensor_tensor(out=mixT[:, bass.ds(i * 2 + 2 * H, 2), :], in0=gr2[:], scalar=0.5, in1=lruH[:],
                                           op0=ALU.mult, op1=ALU.mult), V1, "mixl")
                if not last:
                    add_half(g0 + 4, 0, qT[:])
                    split_units(g0 + 6)
                    add_half(g0 + 5, 1, kT[:])

            with dve.Fori(0, H - 1) as i:
                head(i, False)
            head(H - 1, True)

            def add_residual(V, half):
                for r in range(ROWS):
                    cols = slice(half * HALF, (half + 1) * HALF)
                    bank = 4 * (1 - half) + 2 * r
                    did(v.tensor_tensor(xres[:, r, cols], ps[:, bank:bank + 2, :].rearrange("p a n -> p (a n)"),
                                        xres[:, r, cols], ALU.add), V, f"out{half}_{r}")

            def contraction(src, first_group, bodies, count, V):
                for half in range(2):
                    base = first_group + half * bodies + 1
                    tiles = count + half * bodies * RING + RING
                    if half == 1:
                        for s in range(RING):
                            split_units(base, [s])
                            split_tiles(src, RING, tiles, [s])
                        dve.wait_ge(unit_used, base * RING)
                        add_residual(V, 0)
                    with dve.Fori(half, bodies - 1) as b:
                        for s in range(RING):
                            split_units(b + base, [s])
                            split_tiles(src, b * RING + RING, b * RING + tiles, [s])
                    for s in range(RING):
                        if base + bodies - 1 < G_END:
                            split_units(base + bodies - 1, [s])
                        if half == 0:
                            split_tiles(src, 0, tiles + (bodies - 1) * RING, [s])
                dve.wait_ge(unit_used, (first_group + 2 * bodies) * RING + RING)
                add_residual(V, 1)

            contraction(mixT, G_OUT, OUT_BODIES, 0, V2)
            normalise(A2, V2)
            for b in range(KT // 2):
                transposed_lo(A2, V2, PAR_GFFN, b)
            did(v.memset(fg[:, :, 0:FTAPS - 1], 0.0), V2, "fpad")
            after(dve, V2, "fpad")

            def gate_post(n, j):
                def fpar(b, k):
                    return par[:, bass.ds(j * (2 * FFN_PAR) + (PAR_FFN + b * FFN_PAR + k), 1)]

                add_half(n, 0, fg[:, :, FTAPS - 1:])
                dve.wait_ge(group_free, freed(n))
                for k in range(FTAPS):
                    for b in range(2):
                        tap = fg[:, b, k:k + S]
                        if k == 0:
                            did(v.tensor_scalar(fc[:, b, :], tap, fpar(b, k), fpar(b, FTAPS), ALU.mult, ALU.add),
                                V3, f"c{b}_{k}")
                        else:
                            after(dve, V3, f"c{b}_{k - 1}", j)
                            did(v.scalar_tensor_tensor(out=fc[:, b, :], in0=tap, scalar=fpar(b, k), in1=fc[:, b, :],
                                                       op0=ALU.mult, op1=ALU.add), V3, f"c{b}_{k}")

            def up_post(n, j):
                add_half(n, 1, fu[:])
                dve.wait_ge(group_free, freed(n))
                after(dve, A3, "silu", j)
                did(v.tensor_tensor(act[:, bass.ds(j * 2, 2), :], fu[:], fs[:], ALU.mult), V3, "act")

            n_up = G_UP - NOT_BANKED
            split_units(G_UP + 1)
            gate_post(n_up, 0)
            with dve.Fori(0, UP_ITERS - 1) as j:
                split_units(j * 2 + (G_UP + 2))
                up_post(j * 2 + (n_up + 1), j)
                split_units(j * 2 + (G_UP + 3))
                gate_post(j * 2 + (n_up + 2), j + 1)
            for s in range(RING):
                split_units(G_DOWN, [s])
                split_tiles(act, 0, 2 * KT, [s])
            up_post(n_up + 2 * UP_ITERS - 1, UP_ITERS - 1)
            contraction(act, G_DOWN, DOWN_BODIES, 2 * KT, V4)
            dve.wait_ge(gfin_landed, 16)
            norm_scale(A4, V4)
            for r in range(ROWS):
                cols = slice(HALF, 2 * HALF)
                did(v.scalar_tensor_tensor(out=xn[:, r, cols], in0=xres[:, r, cols], scalar=small[:, RSTD + r:RSTD + r + 1],
                                           in1=gfin[:, cols], op0=ALU.mult, op1=ALU.mult), V4, f"y{r}")

        @block.gpsimd
        def _(pool):
            pool.dma_start(cst[:], const_in).then_inc(par_landed, 16)
            pool.dma_start(par[:], par_in).then_inc(par_landed, 16)
            pool.dma_start(sel[:], sel_in).then_inc(par_landed, 16)
            pool.wait_ge(x_landed[2 * ROWS - 1], 16)
            pool.dma_start(gw, gate_w.rearrange("p (k n) -> p k n", k=KT)).then_inc(gate_landed, 16)
            after(pool, V0, "gw_lo")
            pool.dma_start(gfin[:], gfin_in.to_broadcast([P, D])).then_inc(gfin_landed, 16)
            pool.wait_ge(par_landed, 48)
            with pool.Fori(0, H) as i:
                after(pool, A1, "decay", i)
                for n, col in enumerate((0, S)):
                    did(nc.gpsimd.tensor_tensor(decay[:, col:col + P], decay[:, col:col + P], tri, ALU.mult), L1, f"mask{n}")
            pool.wait_ge(gfin_landed, 16)
            for r in range(ROWS):
                after(pool, A4, f"sq0_{r}")
                did(nc.gpsimd.tensor_tensor(xn[:, r, 0:HALF], xres[:, r, 0:HALF], gfin[:, 0:HALF], ALU.mult), L4, f"xg{r}")

        @block.tensor
        def _(pe):
            mm = nc.tensor.matmul

            def transpose_bank(V, E, b):
                for r in range(ROWS):
                    after(pe, V, f"xn{r}_{b // 2}")
                if b >= 4:
                    after(pe, V, f"t{b - 4}")
                for n in range(2):
                    for r in range(ROWS):
                        kt = 2 * b + n
                        ins = nc.tensor.transpose(ps[:, 4 + b % 4, n * S + r * P:n * S + (r + 1) * P],
                                                  xn[:, r, kt * P:(kt + 1) * P], ident)
                        if V is V0 and b == 0 and n == 0 and r == 0:
                            ins.then_inc(unit_used, RING)
                did(ins, E, f"t{b}")

            def unit(g, s, pair, rows_out=False):
                pe.wait_ge(lo_ready, g * RING + (s + 1 + RING))
                for c in range(CH):
                    kt = s * CH + c
                    for n in range(2):
                        full, rest = ps[:, 2 * pair + n, :], ps[:, 2 * pair + n, COLS:2 * COLS]
                        cut = slice(n * P, (n + 1) * P)
                        if rows_out:
                            mm(full, xT[:, kt, 0, cut], w[:, s, c, :, :].rearrange("p a n -> p (a n)"),
                               start=kt == 0, stop=False)
                            ins = mm(rest, xT[:, kt, 1, cut], w[:, s, c, 0, :], start=False, stop=kt == KT - 1)
                        else:
                            mm(full, w[:, s, c, 0, cut], xT[:, kt, :, :].rearrange("p a n -> p (a n)"),
                               start=kt == 0, stop=False)
                            ins = mm(rest, w[:, s, c, 1, cut], xT[:, kt, 0, :], start=False, stop=kt == KT - 1)
                ins.then_inc(unit_used, 1)

            def group(g, n_banked, pair, rows_out=False):
                pe.wait_ge(group_free, n_banked + 1)
                for s in range(RING):
                    unit(g, s, pair, rows_out)

            def first_group(V, E, g, n_banked):
                for b in range(4):
                    transpose_bank(V, E, b)
                pe.wait_ge(group_free, n_banked + 1)
                for s in range(RING):
                    after(pe, V, f"t{2 * s + 1}")
                    unit(g, s, 0)
                    if s < 2:
                        transpose_bank(V, E, 2 * s + 4)
                        transpose_bank(V, E, 2 * s + 5)

            pe.wait_ge(par_landed, 48)
            first_group(V0, E0, 0, 0)
            after(pe, V0, "gw_lo")
            for kt in range(KT):
                mm(ps[:, B_SC, :], gwh[:, kt, :], xT[:, kt, :, :].rearrange("p a n -> p (a n)"), start=kt == 0, stop=False)
                ins = mm(ps[:, B_SC, S:2 * S], gwl[:, kt, :], xT[:, kt, 0, :], start=False, stop=kt == KT - 1)
            did(ins, E0, "gates")
            group(1, 1, 1)
            after(pe, V0, "neg_clip")
            for r in range(ROWS):
                did(nc.tensor.transpose(ps[:, 5 + r, 0:H], gdif[:, r * P:(r + 1) * P], cst[0:H, C_ID:C_ID + H]), E0, f"gcol{r}")
            after(pe, V0, "gcol1")
            for h in range(H):
                did(mm(ps[:, 4 + h, :], sel[:, h, :], neg[:].rearrange("p a t -> p (a t)"), start=True, stop=True), E0, f"bc{h}")

            def head(i, last):
                g0 = i * MIX_GROUPS + 2
                group(g0, g0, 0, rows_out=True)
                pe.wait_ge(group_free, freed(g0 - 1))
                after(pe, V1, "arg1", i)
                pe.wait_ge(act_step, A1.after("i_tanh1", i - 1))
                for n in range(2):
                    mm(ps[:, B_SC, 0:S], kT[:, n, 0:P], qT[:, n, :], start=n == 0, stop=n == 1)
                for n in range(2):
                    ins = mm(ps[:, B_SC, S:S + P], kT[:, n, P:S], qT[:, n, P:S], start=n == 0, stop=n == 1)
                did(ins, E1, "scores")
                group(g0 + 1, g0 + 1, 1)
                after(pe, V1, "pT", i)
                pe.wait_ge(group_free, freed(g0))
                for n in range(2):
                    cut = slice(n * P, (n + 1) * P)
                    mm(ps[:, B_PV, n * S:(n + 1) * S], vN[:, 0, cut], pT[:, 0:S], start=True, stop=False)
                    mm(ps[:, B_PV, n * S + P:(n + 1) * S], vN[:, 1, cut], pT[:, S:S + P], start=False, stop=True)
                mm(ps[:, B_DEN, 0:S], ones[:], pT[:, 0:S], start=True, stop=False)
                did(mm(ps[:, B_DEN, P:S], ones[:], pT[:, S:S + P], start=False, stop=True), E1, "pv")
                group(g0 + 2, g0 + 2, 0)
                after(pe, A1, "hsq", i)
                after(pe, V1, "den", i)
                for n in range(2):
                    ins = mm(ps[:, B_DEN, S:2 * S], ones[:], hsq[:, n, :], start=n == 0, stop=n == 1)
                did(ins, E1, "rms")
                pe.wait_ge(group_free, g0 + (3 + 1))
                for s in range(RING):
                    unit(g0 + 3, s, 1)
                    if s == 2:
                        after(pe, V1, f"conv1_{TAPS - 1}", i)
                        pe.wait_ge(lru_w_landed, i * 32 + 32)
                        for bank, k in ((B_R, 0), (B_I, 1)):
                            for n in range(2):
                                ins = mm(ps[:, bank, n * S:(n + 1) * S], lru_w[:, n, k, :], xc[:, n, :], start=True, stop=True)
                        did(ins, E1, "lru")
                if not last:
                    group(g0 + 4, g0 + 4, 0)
                    group(g0 + 5, g0 + 5, 1)

            with pe.Fori(0, H - 1) as i:
                head(i, False)
            head(H - 1, True)

            def contraction(first, bodies, count, banked_before):
                for half in range(2):
                    bank0 = 4 * (1 - half)
                    if half == 1:
                        pe.wait_ge(group_free, banked_before + FREE_AT_START)

                    def body(b, first=False, last=False):
                        for s in range(RING):
                            n_unit = b * RING + s
                            pe.wait_ge(lo_ready, n_unit + ((first + half * bodies) * RING + 1 + RING))
                            pe.wait_ge(a_lo_ready, n_unit + (count + half * bodies * RING + 1))
                            for r in range(ROWS):
                                cut = slice(r * P, (r + 1) * P)
                                for a_part, w_part in ((0, 0), (0, 1), (1, 0)):
                                    for n in range(2):
                                        ins = mm(ps[:, bank0 + 2 * r + n, :], aT[:, s, a_part, cut],
                                                 w[:, s, 2 * n:2 * n + 2, w_part, :],
                                                 start=first and s == 0 and a_part == 0 and w_part == 0,
                                                 stop=last and s == RING - 1 and a_part == 1)
                            ins.then_inc(unit_used, 1)

                    body(0, first=True)
                    with pe.Fori(1, bodies - 1) as b:
                        body(b)
                    body(bodies - 1, last=True)

            after(pe, A1, "i_tanh1", H - 1)
            contraction(G_OUT, OUT_BODIES, 0, G_OUT)
            n_up = G_UP - NOT_BANKED
            first_group(V2, E2, G_UP, n_up)
            with pe.Fori(0, UP_ITERS - 1) as j:
                group(j * 2 + (G_UP + 1), j * 2 + (n_up + 1), 1)
                group(j * 2 + (G_UP + 2), j * 2 + (n_up + 2), 0)
            group(G_DOWN - 1, n_up + 2 * UP_ITERS - 1, 1)
            contraction(G_DOWN, DOWN_BODIES, 2 * KT, G_DOWN - NOT_BANKED)


_WEIGHTS = ["w_in", "w_out", "w_up", "w_down"]


def kernel(**inputs):
    import numpy as np
    import concourse.bacc as bacc
    from concourse.bass_utils import run_bass_kernel_spmd

    a = {k: np.asarray(v) for k, v in inputs.items()}

    def cols(v, n):
        return v.reshape(n, P).T

    lru = np.stack([cols(t, LBLK) for t in (*a["lru_conv_w"][0], a["lru_conv_b"][0], a["lru_ba"][0], a["lru_bx"][0],
                                            a["lru_lambda"][0])], axis=2)
    ffn = np.stack([cols(t, FT) for t in (*a["ffn_conv_w"][0], a["ffn_conv_b"][0])], axis=2)
    bias = np.zeros((P, 1), np.float32)
    bias[0:H, 0] = a["b_gate_m"][0, :H]
    bias[F_ROW:F_ROW + H, 0] = a["b_gate_m"][0, H:]
    par = np.concatenate([cols(a["norm_mix_g"][0], KT), cols(a["norm_ffn_g"][0], KT),
                          cols(a["mlstm_norm_g"][0].reshape(-1), 2 * H),
                          lru.reshape(P, -1), ffn.reshape(P, -1), bias], axis=1)
    gate = np.zeros((P, KT, P), np.float32)
    gate_cols = a["w_in"][0][:, 4 * D_M:4 * D_M + 2 * H].reshape(KT, P, 2 * H).transpose(1, 0, 2)
    gate[:, :, 0:H] = gate_cols[:, :, :H]
    gate[:, :, F_ROW:F_ROW + H] = gate_cols[:, :, H:]
    const = np.zeros((P, NCONST), np.float32)
    const[:, C_ID:C_ID + P] = np.eye(P)
    const[:, C_TRI:C_TRI + P] = np.triu(np.ones((P, P)))
    sel = np.zeros((H, H, P), np.float32)
    for h in range(H):
        sel[h, h] = 1.0

    arrays = {"x": a["x"], **{n: a[n][0] for n in _WEIGHTS}, "wa": a["lru_wa"][0], "wx": a["lru_wx"][0],
              "gate_w": gate.reshape(P, -1), "par": par, "const": const, "sel": sel, "gfin": a["norm_final_g"].reshape(1, D)}
    nc = bacc.Bacc("TRN2", target_bir_lowering=False, num_devices=1)
    in_map, args = {}, []
    for name, array in arrays.items():
        in_map[f"{name}_dram"] = np.ascontiguousarray(array)
        args.append(nc.dram_tensor(f"{name}_dram", array.shape, F32, kind="ExternalInput").ap())
    y = nc.dram_tensor("y_dram", (1, S, D), F32, kind="ExternalOutput").ap()
    hybrid_block(nc, *args, y)
    result = run_bass_kernel_spmd(nc, [in_map], core_ids=[0])
    return result.results[0]["y_dram"]
```

```python
from contextlib import ExitStack

import concourse.bass as bass
from concourse import mybir

F32 = mybir.dt.float32
F32R = mybir.dt.float32r
ALU = mybir.AluOpType
ACT = mybir.ActivationFunctionType

P = 128
D = 2048
S = 256
KT = D // P
ROWS = S // P
H = 4
DH = 256
D_M = H * DH
D_L = D - D_M
LBLK = D_L // P
TAPS = 4
D_FF = 5632
FT = D_FF // P
FTAPS = 3
EPS = 1e-6
LRU_C = 8.0

RING = 4
CH = 4
COLS = 256
HALF = CH * COLS
BANK = 512

MIX_GROUPS = 6
OUT_BODIES = KT // RING
UP_ITERS = D_FF // COLS
DOWN_BODIES = FT // RING
G_MIX = 0
G_OUT = G_MIX + H * MIX_GROUPS
G_UP = G_OUT + 2 * OUT_BODIES
G_DOWN = G_UP + 2 * UP_ITERS
G_END = G_DOWN + 2 * DOWN_BODIES

NOT_BANKED = 2 * OUT_BODIES
FREE_AT_START = 2

PAR_GMIX = 0
PAR_GFFN = PAR_GMIX + KT
PAR_HEAD = PAR_GFFN + KT
PAR_LRU = PAR_HEAD + 2 * H
LRU_PAR = 8
PAR_FFN = PAR_LRU + LBLK * LRU_PAR
FFN_PAR = 4
PAR_GATE = PAR_FFN + FT * FFN_PAR
NPAR = PAR_GATE + 1
F_ROW = 32

C_ID, C_TRI = 0, P
NCONST = 2 * P
SSQ, BASE, STD, C_EPS, RSTD, WARM, C_TINY, SSQ_LAST = 0, 4, 6, 8, 10, 12, 13, 14
PIECES = [[(0, HALF), (HALF, D)], [(0, HALF), (HALF, HALF + BANK), (HALF + BANK, D)]]
WARM_UP = 29
TINY = 1e-34
FLOOR_LN = 47.0


def ssq_col(r, n):
    return SSQ_LAST if n == 2 else SSQ + n * ROWS + r


class Steps:

    def __init__(self, sem, base, names):
        self.sem, self.base, self.names = sem, base, names.split()
        self.n = len(self.names)

    def after(self, name, i=0):
        return i * self.n + (self.base + self.names.index(name) + 1)

    def end(self, iterations=1):
        return self.base + self.n * iterations


def hybrid_block(nc, x, w_in, w_out, w_up, w_down, wa, wx, gate_w, par_in, const_in, gfin_in, out):
    with ExitStack() as ctx:
        def sem(name):
            return ctx.enter_context(nc.semaphore(name))

        def sb(name, shape, dt=F32, where=ctx):
            return where.enter_context(nc.sbuf_tensor(name, shape, dt))

        xres = sb("xres", [P, ROWS, D])
        xn = sb("xn", [P, ROWS, D])
        xT = sb("xT", [P, KT, 2, S], F32R)
        raw = sb("raw", [P, RING, HALF])
        w = sb("w", [P, RING, CH, 2, COLS], F32R)
        aT = sb("aT", [P, RING, 2, S], F32R)
        par = sb("par", [P, NPAR])
        cst = sb("cst", [P, NCONST])
        gfin = sb("gfin", [P, D])
        gw = sb("gw", [P, KT, 2, H])
        small = sb("small", [P, 16])
        ones = sb("ones", [P, P])
        ident = cst[:, C_ID:C_ID + P]
        tri = cst[:, C_TRI:C_TRI + P]

        gate_cols = ExitStack()
        gws = sb("gws", [P, KT, 4, F_ROW], F32R, where=gate_cols)
        gate_cols.close()
        mixer = ExitStack()
        mixT = sb("mixT", [P, KT, S], where=mixer)
        qT = sb("qT", [P, 2, S], where=mixer)
        kT = sb("kT", [P, 2, S], where=mixer)
        vN = sb("vN", [P, ROWS, DH], where=mixer)
        bc = sb("bc", [P, H, 2, S], where=mixer)
        gcol = sb("gcol", [P, ROWS, H], where=mixer)
        decay = sb("decay", [P, 3 * P], where=mixer)
        pT = sb("pT", [P, 3 * P], where=mixer)
        den = sb("den", [P, S], where=mixer)
        hT = sb("hT", [P, 2, S], where=mixer)
        hsq = sb("hsq", [P, 2, S], where=mixer)
        oT = sb("oT", [P, 2, S], where=mixer)
        rstd_h = sb("rstd_h", [P, S], where=mixer)
        xr = sb("xr", [P, 2, S + TAPS - 1], where=mixer)
        xc = sb("xc", [P, 2, S], where=mixer)
        rg = sb("rg", [P, 2, S], where=mixer)
        ig = sb("ig", [P, 2, S], where=mixer)
        lruA = sb("lruA", [P, 2, S], where=mixer)
        lruT = sb("lruT", [P, 2, S], where=mixer)
        lruU = sb("lruU", [P, 2, S], where=mixer)
        lruH = sb("lruH", [P, 2, S], where=mixer)
        gr = sb("gr", [P, 2, S], where=mixer)
        gr2 = sb("gr2", [P, 2, S], where=mixer)
        lru_w = sb("lru_w", [P, 2, 2, P], where=mixer)
        lp = sb("lp", [P, 4, LBLK], where=mixer)
        hg = sb("hg", [P, 2 * H], where=mixer)
        gates = ExitStack()
        grow = sb("grow", [64, S], where=gates)
        gtmp = sb("gtmp", [64, S], where=gates)
        logf = sb("logf", [H, S], where=gates)
        fsum = sb("fsum", [H, S], where=gates)
        gdif = sb("gdif", [H, S], where=gates)
        neg = sb("neg", [H, 2, S], where=gates)
        gates.close()
        mixer.close()
        ffn = ExitStack()
        act = sb("act", [P, FT, S], where=ffn)
        fg = sb("fg", [P, 2, S + FTAPS - 1], where=ffn)
        fc = sb("fc", [P, 2, S], where=ffn)
        fs = sb("fs", [P, 2, S], where=ffn)
        fu = sb("fu", [P, 2, S], where=ffn)
        ffn.close()

        rows_dram = nc.dram_tensor("rows", [H, 2 * S], F32, kind="Internal").ap()
        ps = ctx.enter_context(nc.psum_tensor("ps", [P, 8, BANK], F32))
        B_SC, B_R, B_PV, B_DEN = 4, 5, 6, 7
        B_I = B_SC

        x_landed = {(r, n): sem(f"x_landed{r}_{n}") for r in range(ROWS) for n in range(len(PIECES[r]))}
        par_landed = sem("par_landed")
        gate_landed = sem("gate_landed")
        gfin_landed = sem("gfin_landed")
        lru_w_landed = sem("lru_w_landed")
        rows_stored, bc_landed = sem("rows_stored"), sem("bc_landed")
        raw_landed = [sem(f"raw_landed{s}") for s in range(RING)]
        hi_ready = sem("hi_ready")
        lo_ready = sem("lo_ready")
        unit_used = sem("unit_used")
        group_free = sem("group_free")
        half_copied = sem("half_copied")
        a_hi_ready = sem("a_hi_ready")
        a_lo_ready = sem("a_lo_ready")
        stored = sem("stored")
        act_step, dve_step, pe_step, pool_step = sem("act_step"), sem("dve_step"), sem("pe_step"), sem("pool_step")

        stats_act = "warm sq0_0 sq1_0 sq0_1 std0 "
        norm_dve0 = "rstd0 xn0_0 xn0_1 xn0_2 xn0_3 "
        norm_dve1 = "rstd1 xn1_0 xn1_1 xn1_2 "
        tr_steps = " ".join(f"t{b}" for b in range(KT // 2)) + " "
        norm_act = "sq1_1 sq1_2 std1 t0 t1 t2 t3 xn1_3 t4 t5 t6 t7 "
        out_steps = "out0_0 out1_0 base out0_1 "
        A0 = Steps(act_step, 0, stats_act + norm_act + "gw_hi lam_exp lam_ln gate_half f_exp f_ln floor")
        V0 = Steps(dve_step, 0, "start gw_zero base rstd0 xn0_0 xn0_1 base1 xn0_2 xn0_3 " + norm_dve1 + tr_steps
                   + "gw_lo lam_neg lam_abs lam_relu softplus c_col half_bias nc_col hg gate_bias gate_sum"
                   " f_neg f_abs logf fsum gdif cmax neg_M neg_m neg_clip gcol0 gcol1 pads")
        E0 = Steps(pe_step, 0, tr_steps + "gates gcol0 gcol1")
        A1 = Steps(act_step, A0.end(), "decay hsq rms_std o_tanh r_tanh0 r_tanh1 i_tanh0 i_tanh1 lru_a0 lru_a1 lru_t0 lru_t1 lru_s g_tanh")
        V1 = Steps(dve_step, V0.end(), "arg0 arg1 pT dneg den dsq hvar"
                   " conv0_0 conv1_0 conv0_1 conv1_1 conv0_2 conv1_2 conv0_3 conv1_3 rstd og mix0 mix1"
                   " ux asq w u scan0 scan1 gsq gp gq gh mixl")
        E1 = Steps(pe_step, E0.end(), "scores pv rms lru")
        L1 = Steps(pool_step, 0, "mask0 mask1 nsq")
        EO = Steps(pe_step, E1.end(H), "row0_0 row0_1 row1_1")
        A2 = Steps(act_step, A1.end(H), stats_act + norm_act)
        V2 = Steps(dve_step, V1.end(H), out_steps + norm_dve0 + "out1_1 out1_2 base1 " + norm_dve1 + tr_steps + "fpad")
        E2 = Steps(pe_step, EO.end(), tr_steps)
        A3 = Steps(act_step, A2.end(), "silu")
        V3 = Steps(dve_step, V2.end(), "c0_0 c1_0 c0_1 c1_1 c0_2 c1_2 act")
        ED = Steps(pe_step, E2.end(), "row0_0 row0_1 row1_1")
        A4 = Steps(act_step, A3.end(UP_ITERS), stats_act + "y0_0 y0_1 sq1_1 sq1_2 std1 y1_0 y1_1")
        V4 = Steps(dve_step, V3.end(UP_ITERS), out_steps + "rstd0 y0_2 y0_3 out1_1 out1_2 base1 rstd1 y1_2 y1_3")
        L4 = Steps(pool_step, L1.end(H), "xg0 xg1")

        def freed(n):
            return n + (1 + FREE_AT_START)

        def after(eng, steps, name, i=0):
            eng.wait_ge(steps.sem, steps.after(name, i))

        def did(ins, steps, name, seen={}):
            key = id(steps)
            assert steps.names[seen.get(key, 0) % steps.n] == name, (name, steps.names[seen.get(key, 0) % steps.n])
            seen[key] = seen.get(key, 0) + 1
            ins.then_inc(steps.sem, 1)

        block = ctx.enter_context(nc.Block())

        @block.sync
        def _(sp):
            for r, n in ((0, 0), (1, 0), (0, 1), (1, 1), (1, 2)):
                lo, hi = PIECES[r][n]
                sp.dma_start(xres[:, r, lo:hi], x[0, r * P:(r + 1) * P, lo:hi]).then_inc(x_landed[r, n], 16)

            def load(group, s, src, dst):
                sp.wait_ge(lo_ready, group * RING + s + 1)
                sp.dma_start(dst, src).then_inc(raw_landed[s], 16)

            in_v = w_in.rearrange("(s c p) n -> s p c n", c=CH, p=P)
            up_v = w_up.rearrange("(s c p) n -> s p c n", c=CH, p=P)

            def load_group(group, view, col):
                for s in range(RING):
                    load(group, s, view[s, :, :, bass.ds(col, COLS)],
                         raw[:, s, :].rearrange("p (c n) -> p c n", c=CH))

            def load_body(group, weights, b, half):
                rows = weights.rearrange("(b s p) n -> s p b n", s=RING, p=P)
                for s in range(RING):
                    load(group, s, rows[s, :, bass.ds(b, 1), half * HALF:(half + 1) * HALF],
                         raw[:, s, :].rearrange("p (b n) -> p b n", b=1))

            COL_Q, COL_K, COL_V, COL_O, COL_XR, COL_GR = 0, D_M, 2 * D_M, 3 * D_M, 4 * D_M + 2 * H, 4 * D_M + 2 * H + D_L
            wa_v = wa.rearrange("(i b) k j -> i k b j", b=2)
            wx_v = wx.rearrange("(i b) k j -> i k b j", b=2)

            def load_head(i, last):
                g0 = i * MIX_GROUPS + 2
                for g, col in enumerate((COL_V, COL_O, COL_XR, COL_GR)):
                    load_group(g0 + g, in_v, i * COLS + col)
                    if g == 1:
                        sp.wait_ge(pe_step, E1.after("lru", i - 1))
                        for n, view in enumerate((wa_v, wx_v)):
                            sp.dma_start(lru_w[:, :, n, :], view[bass.ds(i, 1)].rearrange("i k b j -> k (i b) j")).then_inc(lru_w_landed, 16)
                if not last:
                    load_group(g0 + 4, in_v, i * COLS + (COL_Q + COLS))
                    load_group(g0 + 5, in_v, i * COLS + (COL_K + COLS))

            load_group(0, in_v, COL_Q)
            load_group(1, in_v, COL_K)
            with sp.Fori(0, H - 1) as i:
                load_head(i, False)
            load_head(H - 1, True)
            for half in range(2):
                with sp.Fori(0, OUT_BODIES) as b:
                    load_body(b + (G_OUT + half * OUT_BODIES), w_out, b, half)
            with sp.Fori(0, UP_ITERS) as j:
                for g in range(2):
                    load_group(j * 2 + (G_UP + g), up_v, j * COLS + g * D_FF)
            for half in range(2):
                with sp.Fori(0, DOWN_BODIES) as b:
                    load_body(b + (G_DOWN + half * DOWN_BODIES), w_down, b, half)
            yv = out.rearrange("a (r p) (c d) -> (a r) c p d", p=P, d=BANK)
            for r, steps, c in [(r, steps, c) for r in range(ROWS) for steps, c in ((V4, 2), (A4, 0), (V4, 3), (A4, 1))]:
                after(sp, steps, f"y{r}_{c}")
                sp.dma_start(yv[r, c], xn[:, r, c * BANK:(c + 1) * BANK]).then_inc(stored, 16)
            sp.wait_ge(stored, 16 * ROWS * D // BANK)

        @block.scalar
        def _(act_e):
            sc = nc.scalar

            def act_fn(out_, in_, fn=ACT.Copy, **kw):
                return sc.activation(out_, in_, fn, **kw)

            def round_units(group, slots=range(RING)):
                for s in slots:
                    act_e.wait_ge(raw_landed[s], group * 16 + 16)
                    act_e.wait_ge(unit_used, group * RING + s + 1)
                    act_fn(w[:, s, :, 0, :], raw[:, s, :].rearrange("p (c n) -> p c n", c=CH)).then_inc(hi_ready, 1)

            def round_tiles(src, first, slots=range(RING)):
                for s in slots:
                    act_fn(aT[:, s, 0, :], src[:, bass.ds(first + s, 1), :].rearrange("p a n -> p (a n)")).then_inc(a_hi_ready, 1)

            def copy_half(group, pair, dst):
                act_e.wait_ge(unit_used, group * RING + 2 * RING)
                act_fn(dst, ps[:, 2 * pair:2 * pair + 2, 0:COLS]).then_inc(half_copied, 1)

            def squares(A, r, n, V=None):
                if V:
                    after(act_e, V, f"out{r}_{n}")
                else:
                    act_e.wait_ge(x_landed[r, n], 16)
                lo, hi = PIECES[r][n]
                col = ssq_col(r, n)
                did(act_fn(xn[:, r, lo:hi], xres[:, r, lo:hi], ACT.Square, accum_out=small[:, col:col + 1]), A, f"sq{r}_{n}")

            def std(A, V, r):
                n = len(PIECES[r]) - 1
                col = ssq_col(r, n)
                after(act_e, V, "base1" if r else "base")
                after(act_e, A, f"sq{r}_{n}")
                did(act_fn(small[:, STD + r:STD + r + 1], small[:, col:col + 1], ACT.Sqrt, scale=1.0 / D,
                           bias=small[:, BASE + r:BASE + r + 1]), A, f"std{r}")

            def stats(A, V, r, source=None):
                for n in range(1, len(PIECES[r])):
                    squares(A, r, n, source)
                std(A, V, r)

            def warm_sqrt(A):
                did(act_fn(small[:, WARM:WARM + 1], small[:, C_EPS:C_EPS + 1], ACT.Sqrt), A, "warm")

            def normalise(A, c):
                cols = slice(c * BANK, (c + 1) * BANK)
                did(act_fn(xn[:, 1, cols], xres[:, 1, cols], scale=small[:, RSTD + 1:RSTD + 2]), A, f"xn1_{c}")

            def transposed_hi(A, E, gains, b):
                after(act_e, E, f"t{b}")
                for n in range(2):
                    kt = 2 * b + n
                    ins = act_fn(xT[:, kt, 0, :], ps[:, 4 + b % 4, n * S:(n + 1) * S],
                                 scale=par[:, gains + kt:gains + kt + 1])
                did(ins, A, f"t{b}")

            def normalised_hi(A, V, E, gains, prepare):
                for s in range(RING):
                    prepare(s)
                    if s == 2:
                        after(act_e, V, "rstd1")
                        normalise(A, 3)
                    transposed_hi(A, E, gains, 2 * s)
                    transposed_hi(A, E, gains, 2 * s + 1)

            after(act_e, V0, "start")
            warm_sqrt(A0)
            for r in range(ROWS):
                squares(A0, r, 0)
            for r in range(ROWS):
                stats(A0, V0, r)
            act_e.wait_ge(par_landed, 32)
            normalised_hi(A0, V0, E0, PAR_GMIX, lambda s: round_units(0, [s]))
            act_e.wait_ge(gate_landed, 16)
            after(act_e, V0, "gw_zero")
            did(act_fn(gws[:, :, 0:2, 0:H], gw[:]), A0, "gw_hi")
            after(act_e, V0, "lam_abs")
            did(act_fn(lp[:, 2, :], lp[:, 2, :], ACT.Exp), A0, "lam_exp")
            after(act_e, A0, "lam_exp")
            did(act_fn(lp[:, 2, :], lp[:, 2, :], ACT.Ln, bias=1.0), A0, "lam_ln")
            round_units(1)
            copy_half(0, 0, qT[:])
            after(act_e, E0, "gates")
            did(act_fn(grow[:], ps[0:64, B_SC, 0:S]), A0, "gate_half")
            after(act_e, V0, "f_abs")
            did(act_fn(gtmp[F_ROW:F_ROW + H], gtmp[F_ROW:F_ROW + H], ACT.Exp), A0, "f_exp")
            after(act_e, A0, "f_exp")
            did(act_fn(gtmp[F_ROW:F_ROW + H], gtmp[F_ROW:F_ROW + H], ACT.Ln, bias=1.0), A0, "f_ln")
            round_units(2, range(3))
            after(act_e, V0, "neg_clip")
            did(act_fn(neg[:, 1, :], neg[:, 1, :], ACT.Exp), A0, "floor")
            round_units(2, range(3, RING))
            copy_half(1, 1, kT[:])

            def head(i, last):
                g0 = i * MIX_GROUPS + 2
                round_units(g0 + 1)
                after(act_e, V1, "arg1", i)
                did(act_fn(decay[:], decay[:], ACT.Exp), A1, "decay")
                copy_half(g0, 0, vN[:])
                round_units(g0 + 2)
                copy_half(g0 + 1, 1, oT[:])
                after(act_e, E1, "pv", i)
                did(act_fn(hsq[:].rearrange("p a t -> p (a t)"), ps[:, B_PV, :], ACT.Square), A1, "hsq")
                round_units(g0 + 3)
                copy_half(g0 + 2, 0, xr[:, :, TAPS - 1:])
                after(act_e, V1, "hvar", i)
                did(act_fn(rstd_h[:], rstd_h[:], ACT.Sqrt, bias=small[:, C_TINY:C_TINY + 1]), A1, "rms_std")
                act_e.wait_ge(group_free, freed(g0 + 1))
                did(act_fn(oT[:], oT[:], ACT.Tanh, scale=0.5), A1, "o_tanh")
                if last:
                    for s in range(3):
                        round_units(G_OUT, [s])
                        round_tiles(mixT, 0, [s])
                    round_tiles(mixT, 0, [3])
                else:
                    round_units(g0 + 4, range(3))
                after(act_e, E1, "lru", i)
                for n in range(2):
                    did(act_fn(rg[:, n, :], ps[:, B_R, n * S:(n + 1) * S], ACT.Tanh, scale=0.5,
                               bias=lp[:, 0, bass.ds(i * 2 + n, 1)]), A1, f"r_tanh{n}")
                for n in range(2):
                    did(act_fn(ig[:, n, :], ps[:, B_I, n * S:(n + 1) * S], ACT.Tanh, scale=0.5,
                               bias=lp[:, 1, bass.ds(i * 2 + n, 1)]), A1, f"i_tanh{n}")
                after(act_e, A1, "r_tanh1", i)
                for n in range(2):
                    did(act_fn(lruA[:, n, :], rg[:, n, :], ACT.Exp, scale=lp[:, 2, bass.ds(i * 2 + n, 1)],
                               bias=lp[:, 2, bass.ds(i * 2 + n, 1)]), A1, f"lru_a{n}")
                for n in range(2):
                    did(act_fn(lruT[:, n, :], rg[:, n, :], ACT.Tanh, scale=lp[:, 3, bass.ds(i * 2 + n, 1)],
                               bias=lp[:, 3, bass.ds(i * 2 + n, 1)]), A1, f"lru_t{n}")
                round_units(g0 + 4, range(3, RING))
                after(act_e, V1, "w", i)
                did(act_fn(lruT[:], lruT[:], ACT.Sqrt, scale=0.25), A1, "lru_s")
                copy_half(g0 + 3, 1, gr[:])
                if last:
                    for s in range(2):
                        round_units(G_OUT + 1, [s])
                        round_tiles(mixT, RING, [s])
                else:
                    round_units(g0 + 5)
                after(act_e, V1, "gq", i)
                did(act_fn(gr2[:], gr2[:], ACT.Tanh, scale=0.7978845608028654), A1, "g_tanh")
                if last:
                    for s in range(2, RING):
                        round_units(G_OUT + 1, [s])
                        round_tiles(mixT, RING, [s])
                if not last:
                    copy_half(g0 + 4, 0, qT[:])
                    round_units(g0 + 6)
                    copy_half(g0 + 5, 1, kT[:])

            with act_e.Fori(0, H - 1) as i:
                head(i, False)
            head(H - 1, True)

            def contraction(src, first_group, bodies, A, V):
                for half in range(2):
                    base = first_group + half * bodies + 1
                    if half == 1 or src is not mixT:
                        for s in range(RING):
                            round_units(base, [s])
                            round_tiles(src, RING, [s])
                    if half == 1:
                        warm_sqrt(A)
                        for r in range(ROWS):
                            squares(A, r, 0, V)
                    with act_e.Fori(1, bodies - 1) as b:
                        for s in range(RING):
                            round_units(b + base, [s])
                            round_tiles(src, b * RING + RING, [s])
                    if half == 0:
                        for s in range(RING):
                            round_units(base + bodies - 1, [s])
                            round_tiles(src, 0, [s])

            after(act_e, V1, "mixl", H - 1)
            contraction(mixT, G_OUT, OUT_BODIES, A2, V2)
            stats(A2, V2, 0, V2)
            round_units(G_UP, range(3))
            stats(A2, V2, 1, V2)
            normalised_hi(A2, V2, E2, PAR_GFFN, lambda s: round_units(G_UP, [s + 1] if s == 2 else []))

            def gate_post(group, j):
                copy_half(group, 0, fg[:, :, FTAPS - 1:])
                after(act_e, V3, "c1_2", j)
                did(act_fn(fs[:], fc[:], ACT.Silu), A3, "silu")

            round_units(G_UP + 1)
            gate_post(G_UP, 0)
            with act_e.Fori(0, UP_ITERS - 1) as j:
                round_units(j * 2 + (G_UP + 2))
                act_e.wait_ge(dve_step, V3.after("act", j - 1))
                copy_half(j * 2 + (G_UP + 1), 1, fu[:])
                round_units(j * 2 + (G_UP + 3))
                gate_post(j * 2 + (G_UP + 2), j + 1)
            for s in range(RING):
                round_units(G_DOWN, [s])
                round_tiles(act, 0, [s])
            copy_half(G_DOWN - 1, 1, fu[:])
            after(act_e, V3, "act", UP_ITERS - 1)
            contraction(act, G_DOWN, DOWN_BODIES, A4, V4)
            for r in range(ROWS):
                stats(A4, V4, r, V4)
                after(act_e, V4, f"rstd{r}")
                after(act_e, L4, f"xg{r}")
                for n in range(2):
                    cols = slice(n * BANK, (n + 1) * BANK)
                    did(act_fn(xn[:, r, cols], xn[:, r, cols], scale=small[:, RSTD + r:RSTD + r + 1]), A4, f"y{r}_{n}")

        @block.vector
        def _(dve):
            v = nc.vector

            def split_units(group, slots=range(RING)):
                for s in slots:
                    dve.wait_ge(hi_ready, group * RING + s + 1)
                    v.tensor_tensor(w[:, s, :, 1, :], raw[:, s, :].rearrange("p (c n) -> p c n", c=CH),
                                    w[:, s, :, 0, :], ALU.subtract).then_inc(lo_ready, 1)

            def split_tiles(src, first, count, slots=range(RING)):
                for s in slots:
                    dve.wait_ge(a_hi_ready, count + s + 1)
                    v.tensor_tensor(aT[:, s, 1, :], src[:, bass.ds(first + s, 1), :].rearrange("p a n -> p (a n)"),
                                    aT[:, s, 0, :], ALU.subtract).then_inc(a_lo_ready, 1)

            def add_half(n, pair, dst):
                dve.wait_ge(half_copied, n + 1)
                v.tensor_tensor(dst, ps[:, 2 * pair:2 * pair + 2, COLS:2 * COLS], dst, ALU.add).then_inc(group_free, 1)

            def norm_base(A, V):
                after(dve, A, "sq1_0")
                did(v.tensor_scalar(small[:, BASE:BASE + ROWS], small[:, SSQ:SSQ + ROWS], 1.0 / D, EPS, ALU.mult, ALU.add), V, "base")

            def norm_scale(A, V, r):
                after(dve, A, f"std{r}")
                did(v.reciprocal(small[:, RSTD + r:RSTD + r + 1], small[:, STD + r:STD + r + 1]), V, f"rstd{r}")
                after(dve, V, f"rstd{r}")

            def norm_base1(A, V):
                after(dve, A, "sq1_1")
                n = ssq_col(1, 1)
                did(v.scalar_tensor_tensor(out=small[:, BASE + 1:BASE + 2], in0=small[:, n:n + 1], scalar=1.0 / D,
                                           in1=small[:, BASE + 1:BASE + 2], op0=ALU.mult, op1=ALU.add), V, "base1")

            def normalise(A, V, r, pieces):
                if 0 in pieces:
                    norm_scale(A, V, r)
                for c in pieces:
                    cols = slice(c * BANK, (c + 1) * BANK)
                    did(v.tensor_scalar(xn[:, r, cols], xres[:, r, cols], small[:, RSTD + r:RSTD + r + 1], None, ALU.mult), V, f"xn{r}_{c}")

            def transposed_lo(A, V, gains, b):
                after(dve, A, f"t{b}")
                for n in range(2):
                    kt = 2 * b + n
                    ins = v.scalar_tensor_tensor(out=xT[:, kt, 1, :], in0=ps[:, 4 + b % 4, n * S:(n + 1) * S],
                                                 scalar=par[:, gains + kt:gains + kt + 1], in1=xT[:, kt, 0, :],
                                                 op0=ALU.mult, op1=ALU.subtract)
                did(ins, V, f"t{b}")

            v.memset(small[:], 0.0).then_inc(lo_ready, RING)
            dve.wait_ge(lo_ready, RING)
            v.memset(small[:, C_EPS + 1:C_EPS + 2], 0.0).then_inc(group_free, FREE_AT_START)
            v.memset(ones[:], 1.0)
            v.memset(small[:, C_TINY:C_TINY + 1], TINY)
            did(v.memset(small[:, C_EPS:C_EPS + 1], EPS), V0, "start")
            did(v.memset(gws[:].bitcast(F32), 0.0), V0, "gw_zero")
            norm_base(A0, V0)
            normalise(A0, V0, 0, (0, 1))
            norm_base1(A0, V0)
            normalise(A0, V0, 0, (2, 3))
            normalise(A0, V0, 1, (0, 1, 2))
            dve.wait_ge(par_landed, 32)
            for s in range(RING):
                split_units(0, [s])
                transposed_lo(A0, V0, PAR_GMIX, 2 * s)
                transposed_lo(A0, V0, PAR_GMIX, 2 * s + 1)
            after(dve, A0, "gw_hi")
            did(v.tensor_tensor(gws[:, :, 2:4, 0:H], gw[:], gws[:, :, 0:2, 0:H], ALU.subtract), V0, "gw_lo")

            lru_par = par[:, PAR_LRU:PAR_LRU + LBLK * LRU_PAR].rearrange("p (b n) -> p n b", n=LRU_PAR)
            lam = lru_par[:, 7, :]
            did(v.tensor_scalar(lp[:, 3, :], lam, -1.0, None, ALU.mult), V0, "lam_neg")
            after(dve, V0, "lam_neg")
            did(v.tensor_tensor(lp[:, 2, :], lp[:, 3, :], lam, ALU.min), V0, "lam_abs")
            after(dve, V0, "lam_abs")
            did(v.tensor_scalar(lp[:, 3, :], lp[:, 3, :], 0.0, None, ALU.max), V0, "lam_relu")
            after(dve, A0, "lam_ln")
            after(dve, V0, "lam_relu")
            did(v.tensor_tensor(lp[:, 3, :], lp[:, 3, :], lp[:, 2, :], ALU.add), V0, "softplus")
            after(dve, V0, "softplus")
            did(v.tensor_scalar(lp[:, 2, :], lp[:, 3, :], -LRU_C / 2, None, ALU.mult), V0, "c_col")
            did(v.tensor_scalar(lp[:, 0:2, :], lru_par[:, 5:7, :], 0.5, None, ALU.mult), V0, "half_bias")
            after(dve, V0, "half_bias")
            did(v.tensor_scalar(lp[:, 3, :], lp[:, 3, :], LRU_C / 2, None, ALU.mult), V0, "nc_col")
            did(v.tensor_scalar(hg[:], par[:, PAR_HEAD:PAR_HEAD + 2 * H], 0.5, None, ALU.mult), V0, "hg")

            split_units(1)
            add_half(0, 0, qT[:])
            frow = slice(F_ROW, F_ROW + H)
            after(dve, A0, "gate_half")
            did(v.scalar_tensor_tensor(out=grow[:], in0=ps[0:64, B_SC, S:2 * S], scalar=par[0:64, PAR_GATE:PAR_GATE + 1],
                                       in1=grow[:], op0=ALU.add, op1=ALU.add), V0, "gate_bias")
            after(dve, V0, "gate_bias")
            did(v.tensor_tensor(grow[:], ps[64:128, B_SC, 0:S], grow[:], ALU.add), V0, "gate_sum")
            after(dve, V0, "gate_sum")
            did(v.tensor_scalar(gtmp[frow], grow[frow], -1.0, None, ALU.mult), V0, "f_neg")
            after(dve, V0, "f_neg")
            did(v.tensor_tensor(gtmp[frow], gtmp[frow], grow[frow], ALU.min), V0, "f_abs")
            after(dve, A0, "f_ln")
            did(v.scalar_tensor_tensor(out=logf[:], in0=grow[frow], scalar=0.0, in1=gtmp[frow],
                                       op0=ALU.min, op1=ALU.subtract), V0, "logf")
            after(dve, V0, "logf")
            one_row = ones[0:H, 0:1].to_broadcast([H, S])
            did(v.tensor_tensor_scan(fsum[:], one_row, logf[:], 0.0, ALU.mult, ALU.add), V0, "fsum")
            after(dve, V0, "fsum")
            did(v.tensor_tensor(gdif[:], grow[0:H], fsum[:], ALU.subtract), V0, "gdif")
            after(dve, V0, "gdif")
            did(v.tensor_tensor_scan(logf[:], one_row, gdif[:], 0.0, ALU.mult, ALU.max), V0, "cmax")
            after(dve, V0, "cmax")
            did(v.tensor_scalar(neg[:, 0, :], logf[:], -1.0, None, ALU.mult), V0, "neg_M")
            after(dve, V0, "neg_M")
            did(v.tensor_tensor(neg[:, 1, :], neg[:, 0, :], fsum[:], ALU.subtract), V0, "neg_m")
            after(dve, V0, "neg_m")
            did(v.tensor_scalar(neg[:, 1, :], neg[:, 1, :], FLOOR_LN, None, ALU.min), V0, "neg_clip")
            split_units(2)
            add_half(1, 1, kT[:])
            for r in range(ROWS):
                after(dve, E0, f"gcol{r}")
                did(v.tensor_copy(gcol[:, r, :], ps[:, 5 + r, 0:H]), V0, f"gcol{r}")
            did(v.memset(xr[:, :, 0:TAPS - 1], 0.0), V0, "pads")
            after(dve, V0, "pads")

            def head(i, last):
                g0 = i * MIX_GROUPS + 2

                def lpar(n, k):
                    return par[:, bass.ds(i * (2 * LRU_PAR) + (PAR_LRU + n * LRU_PAR + k), 1)]

                def chain(name):
                    after(dve, V1, name, i)

                split_units(g0 + 1)
                dve.wait_ge(bc_landed, 16 * H)
                did(v.tensor_scalar(decay[:, 0:S], bc[:, bass.ds(i, 1), 0, :].rearrange("p a t -> p (a t)"),
                                    gcol[:, 0, bass.ds(i, 1)], 0.0, ALU.add, ALU.min), V1, "arg0")
                did(v.tensor_scalar(decay[:, S:S + P], bc[:, bass.ds(i, 1), 0, P:S].rearrange("p a t -> p (a t)"),
                                    gcol[:, 1, bass.ds(i, 1)], 0.0, ALU.add, ALU.min), V1, "arg1")
                add_half(g0, 0, vN[:])
                after(dve, L1, "mask1", i)
                after(dve, E1, "scores", i)
                did(v.scalar_tensor_tensor(out=pT[:], in0=ps[:, B_SC, 0:3 * P], scalar=DH ** -0.5, in1=decay[:],
                                           op0=ALU.mult, op1=ALU.mult), V1, "pT")
                split_units(g0 + 2)
                add_half(g0 + 1, 1, oT[:])
                after(dve, E1, "pv", i)
                did(v.scalar_tensor_tensor(out=den[:], in0=ps[:, B_DEN, 0:S], scalar=-1.0,
                                           in1=bc[:, bass.ds(i, 1), 1, :].rearrange("p a t -> p (a t)"),
                                           op0=ALU.mult, op1=ALU.max), V1, "dneg")
                chain("dneg")
                did(v.tensor_tensor(den[:], ps[:, B_DEN, 0:S], den[:], ALU.max), V1, "den")
                chain("den")
                did(v.scalar_tensor_tensor(out=den[:], in0=den[:], scalar=EPS, in1=den[:], op0=ALU.mult, op1=ALU.mult), V1, "dsq")
                split_units(g0 + 3)
                add_half(g0 + 2, 0, xr[:, :, TAPS - 1:])
                after(dve, E1, "rms", i)
                chain("dsq")
                did(v.scalar_tensor_tensor(out=rstd_h[:], in0=ps[:, B_DEN, S:2 * S], scalar=1.0 / DH, in1=den[:],
                                           op0=ALU.mult, op1=ALU.add), V1, "hvar")
                dve.wait_ge(group_free, freed(g0 + 2))
                for k in range(TAPS):
                    for n in range(2):
                        tap = xr[:, n, k:k + S]
                        if k == 0:
                            did(v.tensor_scalar(xc[:, n, :], tap, lpar(n, k), lpar(n, TAPS), ALU.mult, ALU.add),
                                V1, f"conv{n}_{k}")
                        else:
                            chain(f"conv{n}_{k - 1}")
                            did(v.scalar_tensor_tensor(out=xc[:, n, :], in0=tap, scalar=lpar(n, k), in1=xc[:, n, :],
                                                       op0=ALU.mult, op1=ALU.add), V1, f"conv{n}_{k}")
                after(dve, A1, "rms_std", i)
                did(v.reciprocal(rstd_h[:], rstd_h[:]), V1, "rstd")
                after(dve, A1, "o_tanh", i)
                did(v.scalar_tensor_tensor(out=hT[:].rearrange("p a t -> p (a t)"), in0=oT[:].rearrange("p a t -> p (a t)"),
                                           scalar=1.0, in1=ps[:, B_PV, :], op0=ALU.add, op1=ALU.mult), V1, "og")
                chain("og")
                for n in range(2):
                    did(v.scalar_tensor_tensor(out=mixT[:, bass.ds(i * 2 + n, 1), :].rearrange("p a t -> p (a t)"),
                                               in0=hT[:, n, :], scalar=hg[:, bass.ds(i * 2 + n, 1)], in1=rstd_h[:],
                                               op0=ALU.mult, op1=ALU.mult), V1, f"mix{n}")
                if last:
                    for s in range(3):
                        split_units(G_OUT, [s])
                        split_tiles(mixT, 0, 0, [s])
                    split_tiles(mixT, 0, 0, [3])
                else:
                    split_units(g0 + 4, range(3))
                after(dve, A1, "i_tanh1", i)
                did(v.scalar_tensor_tensor(out=lruU[:], in0=ig[:], scalar=1.0, in1=xc[:], op0=ALU.add, op1=ALU.mult), V1, "ux")
                after(dve, A1, "lru_a1", i)
                did(v.tensor_tensor(lruH[:], lruA[:], lruA[:], ALU.mult), V1, "asq")
                after(dve, A1, "lru_t1", i)
                chain("asq")
                did(v.scalar_tensor_tensor(out=lruT[:], in0=lruH[:], scalar=1.0, in1=lruT[:], op0=ALU.add, op1=ALU.mult), V1, "w")
                split_units(g0 + 4, range(3, RING))
                after(dve, A1, "lru_s", i)
                did(v.tensor_tensor(lruU[:], lruU[:], lruT[:], ALU.mult), V1, "u")
                chain("u")
                for n in range(2):
                    did(v.tensor_tensor_scan(lruH[:, n, :], lruA[:, n, :], lruU[:, n, :], 0.0, ALU.mult, ALU.add),
                        V1, f"scan{n}")
                add_half(g0 + 3, 1, gr[:])
                dve.wait_ge(group_free, freed(g0 + 3))
                did(v.tensor_tensor(gr2[:], gr[:], gr[:], ALU.mult), V1, "gsq")
                chain("gsq")
                did(v.tensor_scalar(gr2[:], gr2[:], 0.044715, 1.0, ALU.mult, ALU.add), V1, "gp")
                chain("gp")
                did(v.tensor_tensor(gr2[:], gr2[:], gr[:], ALU.mult), V1, "gq")
                if last:
                    for s in range(2):
                        split_units(G_OUT + 1, [s])
                        split_tiles(mixT, RING, RING, [s])
                else:
                    split_units(g0 + 5)
                after(dve, A1, "g_tanh", i)
                did(v.scalar_tensor_tensor(out=gr2[:], in0=gr2[:], scalar=1.0, in1=gr[:], op0=ALU.add, op1=ALU.mult), V1, "gh")
                chain("gh")
                did(v.scalar_tensor_tensor(out=mixT[:, bass.ds(i * 2 + 2 * H, 2), :], in0=gr2[:], scalar=0.5, in1=lruH[:],
                                           op0=ALU.mult, op1=ALU.mult), V1, "mixl")
                if last:
                    for s in range(2, RING):
                        split_units(G_OUT + 1, [s])
                        split_tiles(mixT, RING, RING, [s])
                else:
                    add_half(g0 + 4, 0, qT[:])
                    split_units(g0 + 6)
                    add_half(g0 + 5, 1, kT[:])

            with dve.Fori(0, H - 1) as i:
                head(i, False)
            head(H - 1, True)

            def add_residual(V, E, first_group, bodies, r, n):
                half = min(n, 1)
                if r == 0 or n == 1:
                    after(dve, E, f"row{r}_{half}")
                else:
                    dve.wait_ge(unit_used, (first_group + (half + 1) * bodies) * RING + RING)
                lo, hi = PIECES[r][n]
                bank = 4 * (1 - half) + 2 * r + (n == 2)
                did(v.tensor_tensor(xres[:, r, lo:hi], ps[:, bank:bank + (hi - lo) // BANK, :].rearrange("p a n -> p (a n)"),
                                    xres[:, r, lo:hi], ALU.add), V, f"out{r}_{n}")

            def contraction(src, first_group, bodies, count, A, V, E):
                for half in range(2):
                    base = first_group + half * bodies + 1
                    tiles = count + half * bodies * RING + RING
                    if half == 1 or src is not mixT:
                        for s in range(RING):
                            split_units(base, [s])
                            split_tiles(src, RING, tiles, [s])
                    if half == 1:
                        for r in range(ROWS):
                            add_residual(V, E, first_group, bodies, r, 0)
                    with dve.Fori(1, bodies - 1) as b:
                        for s in range(RING):
                            split_units(b + base, [s])
                            split_tiles(src, b * RING + RING, b * RING + tiles, [s])
                    if half == 1:
                        norm_base(A, V)
                    if half == 0:
                        for s in range(RING):
                            split_units(base + bodies - 1, [s])
                            split_tiles(src, 0, tiles + (bodies - 1) * RING, [s])

            contraction(mixT, G_OUT, OUT_BODIES, 0, A2, V2, EO)
            add_residual(V2, EO, G_OUT, OUT_BODIES, 0, 1)
            normalise(A2, V2, 0, range(4))
            for n in (1, 2):
                add_residual(V2, EO, G_OUT, OUT_BODIES, 1, n)
            norm_base1(A2, V2)
            normalise(A2, V2, 1, (0, 1, 2))
            split_units(G_UP, [0])
            for b in range(KT // 2):
                if b in (2, 4, 6):
                    split_units(G_UP, [b // 2])
                transposed_lo(A2, V2, PAR_GFFN, b)
            did(v.memset(fg[:, :, 0:FTAPS - 1], 0.0), V2, "fpad")
            after(dve, V2, "fpad")

            def gate_post(n, j):
                def fpar(b, k):
                    return par[:, bass.ds(j * (2 * FFN_PAR) + (PAR_FFN + b * FFN_PAR + k), 1)]

                add_half(n, 0, fg[:, :, FTAPS - 1:])
                dve.wait_ge(group_free, freed(n))
                for k in range(FTAPS):
                    for b in range(2):
                        tap = fg[:, b, k:k + S]
                        if k == 0:
                            did(v.tensor_scalar(fc[:, b, :], tap, fpar(b, k), fpar(b, FTAPS), ALU.mult, ALU.add),
                                V3, f"c{b}_{k}")
                        else:
                            after(dve, V3, f"c{b}_{k - 1}", j)
                            did(v.scalar_tensor_tensor(out=fc[:, b, :], in0=tap, scalar=fpar(b, k), in1=fc[:, b, :],
                                                       op0=ALU.mult, op1=ALU.add), V3, f"c{b}_{k}")

            def up_post(n, j):
                add_half(n, 1, fu[:])
                dve.wait_ge(group_free, freed(n))
                after(dve, A3, "silu", j)
                did(v.tensor_tensor(act[:, bass.ds(j * 2, 2), :], fu[:], fs[:], ALU.mult), V3, "act")

            n_up = G_UP - NOT_BANKED
            split_units(G_UP + 1)
            gate_post(n_up, 0)
            with dve.Fori(0, UP_ITERS - 1) as j:
                split_units(j * 2 + (G_UP + 2))
                up_post(j * 2 + (n_up + 1), j)
                split_units(j * 2 + (G_UP + 3))
                gate_post(j * 2 + (n_up + 2), j + 1)
            for s in range(RING):
                split_units(G_DOWN, [s])
                split_tiles(act, 0, 2 * KT, [s])
            up_post(n_up + 2 * UP_ITERS - 1, UP_ITERS - 1)
            contraction(act, G_DOWN, DOWN_BODIES, 2 * KT, A4, V4, ED)
            dve.wait_ge(gfin_landed, 16)
            for r in range(ROWS):
                for n in range(1, len(PIECES[r])):
                    add_residual(V4, ED, G_DOWN, DOWN_BODIES, r, n)
                if r == 1:
                    norm_base1(A4, V4)
                norm_scale(A4, V4, r)
                for n in (2, 3):
                    cols = slice(n * BANK, (n + 1) * BANK)
                    did(v.scalar_tensor_tensor(out=xn[:, r, cols], in0=xres[:, r, cols], scalar=small[:, RSTD + r:RSTD + r + 1],
                                               in1=gfin[:, cols], op0=ALU.mult, op1=ALU.mult), V4, f"y{r}_{n}")

        @block.gpsimd
        def _(pool):
            pool.dma_start(cst[:], const_in).then_inc(par_landed, 16)
            pool.dma_start(par[:], par_in).then_inc(par_landed, 16)
            pool.dma_start(gw[:], gate_w).then_inc(gate_landed, 16)
            pool.wait_ge(par_landed, 32)
            after(pool, A0, "floor")
            pool.dma_start(rows_dram, neg[:].rearrange("h a t -> h (a t)")).then_inc(rows_stored, 16)
            pool.wait_ge(rows_stored, 16)
            for h in range(H):
                pool.dma_start(bc[:, h].rearrange("p a t -> p (a t)"), rows_dram[h:h + 1].to_broadcast([P, 2 * S])).then_inc(bc_landed, 16)
            with pool.Fori(0, H) as i:
                after(pool, A1, "decay", i)
                for n, col in enumerate((0, S)):
                    did(nc.gpsimd.tensor_tensor(decay[:, col:col + P], decay[:, col:col + P], tri, ALU.mult), L1, f"mask{n}")
                after(pool, A1, "hsq", i)
                did(nc.gpsimd.tensor_tensor(hsq[:, 0, :], hsq[:, 0, :], hsq[:, 1, :], ALU.add), L1, "nsq")
            pool.dma_start(gfin[:], gfin_in.to_broadcast([P, D])).then_inc(gfin_landed, 16)
            pool.wait_ge(gfin_landed, 16)
            for r in range(ROWS):
                after(pool, A4, f"sq{r}_0")
                did(nc.gpsimd.tensor_tensor(xn[:, r, 0:HALF], xres[:, r, 0:HALF], gfin[:, 0:HALF], ALU.mult), L4, f"xg{r}")

        @block.tensor
        def _(pe):
            mm = nc.tensor.matmul

            def transpose_bank(A, V, E, b):
                c = b // 2
                after(pe, V, f"xn0_{c}")
                after(pe, A if c == 3 else V, f"xn1_{c}")
                if b >= 4:
                    after(pe, V, f"t{b - 4}")
                for n in range(2):
                    for r in range(ROWS):
                        kt = 2 * b + n
                        ins = nc.tensor.transpose(ps[:, 4 + b % 4, n * S + r * P:n * S + (r + 1) * P],
                                                  xn[:, r, kt * P:(kt + 1) * P], ident)
                did(ins, E, f"t{b}")

            def unit(g, s, pair, rows_out=False, tiles=None):
                pe.wait_ge(lo_ready, g * RING + (s + 1 + RING))
                for c in range(CH):
                    kt = s * CH + c
                    if tiles and c % 2 == 0:
                        after(pe, tiles, f"t{kt // 2}")
                    for n in range(2):
                        full, rest = ps[:, 2 * pair + n, :], ps[:, 2 * pair + n, COLS:2 * COLS]
                        cut = slice(n * P, (n + 1) * P)
                        if rows_out:
                            mm(full, xT[:, kt, 0, cut], w[:, s, c, :, :].rearrange("p a n -> p (a n)"),
                               start=kt == 0, stop=False)
                            ins = mm(rest, xT[:, kt, 1, cut], w[:, s, c, 0, :], start=False, stop=kt == KT - 1)
                        else:
                            mm(full, w[:, s, c, 0, cut], xT[:, kt, :, :].rearrange("p a n -> p (a n)"),
                               start=kt == 0, stop=False)
                            ins = mm(rest, w[:, s, c, 1, cut], xT[:, kt, 0, :], start=False, stop=kt == KT - 1)
                ins.then_inc(unit_used, 1)

            def group(g, n_banked, pair, rows_out=False):
                pe.wait_ge(group_free, n_banked + 1)
                for s in range(RING):
                    unit(g, s, pair, rows_out)

            def first_group(A, V, E, g, n_banked):
                for b in range(4):
                    transpose_bank(A, V, E, b)
                pe.wait_ge(group_free, n_banked + 1)
                for s in range(RING):
                    unit(g, s, 0, tiles=V)
                    if s < 2:
                        transpose_bank(A, V, E, 2 * s + 4)
                        transpose_bank(A, V, E, 2 * s + 5)

            after(pe, V0, "start")
            for n in range(WARM_UP):
                ins = mm(ps[:, B_DEN, 0:P], ones[:], ones[:], start=True, stop=True)
                if n == 0:
                    ins.then_inc(unit_used, RING)
            pe.wait_ge(par_landed, 32)
            first_group(A0, V0, E0, 0, 0)
            after(pe, V0, "gw_lo")
            for kt in range(KT):
                ins = mm(ps[:, B_SC, :], gws[:, kt, :, :].rearrange("p a n -> p (a n)"),
                         xT[:, kt, :, :].rearrange("p a n -> p (a n)"), start=kt == 0, stop=kt == KT - 1)
            did(ins, E0, "gates")
            group(1, 1, 1)
            after(pe, V0, "gdif")
            for r in range(ROWS):
                did(nc.tensor.transpose(ps[:, 5 + r, 0:H], gdif[:, r * P:(r + 1) * P], cst[0:H, C_ID:C_ID + H]), E0, f"gcol{r}")

            def head(i, last):
                g0 = i * MIX_GROUPS + 2
                group(g0, g0, 0, rows_out=True)
                after(pe, V0, "gcol1")
                pe.wait_ge(group_free, freed(g0 - 1))
                pe.wait_ge(act_step, A1.after("i_tanh1", i - 1))
                for n in range(2):
                    mm(ps[:, B_SC, 0:S], kT[:, n, 0:P], qT[:, n, :], start=n == 0, stop=n == 1)
                for n in range(2):
                    ins = mm(ps[:, B_SC, S:S + P], kT[:, n, P:S], qT[:, n, P:S], start=n == 0, stop=n == 1)
                did(ins, E1, "scores")
                group(g0 + 1, g0 + 1, 1)
                after(pe, V1, "pT", i)
                pe.wait_ge(group_free, freed(g0))
                for n in range(2):
                    cut = slice(n * P, (n + 1) * P)
                    mm(ps[:, B_PV, n * S:(n + 1) * S], vN[:, 0, cut], pT[:, 0:S], start=True, stop=False)
                    mm(ps[:, B_PV, n * S + P:(n + 1) * S], vN[:, 1, cut], pT[:, S:S + P], start=False, stop=True)
                mm(ps[:, B_DEN, 0:S], ones[:], pT[:, 0:S], start=True, stop=False)
                did(mm(ps[:, B_DEN, P:S], ones[:], pT[:, S:S + P], start=False, stop=True), E1, "pv")
                group(g0 + 2, g0 + 2, 0)
                after(pe, L1, "nsq", i)
                after(pe, V1, "den", i)
                did(mm(ps[:, B_DEN, S:2 * S], ones[:], hsq[:, 0, :], start=True, stop=True), E1, "rms")
                pe.wait_ge(group_free, g0 + (3 + 1))
                for s in range(RING):
                    unit(g0 + 3, s, 1)
                    if s == 2:
                        after(pe, V1, f"conv1_{TAPS - 1}", i)
                        pe.wait_ge(lru_w_landed, i * 32 + 32)
                        for bank, k in ((B_R, 0), (B_I, 1)):
                            for n in range(2):
                                ins = mm(ps[:, bank, n * S:(n + 1) * S], lru_w[:, n, k, :], xc[:, n, :], start=True, stop=True)
                        did(ins, E1, "lru")
                if not last:
                    group(g0 + 4, g0 + 4, 0)
                    group(g0 + 5, g0 + 5, 1)

            with pe.Fori(0, H - 1) as i:
                head(i, False)
            head(H - 1, True)

            def contraction(first, bodies, count, banked_before, E):
                for half in range(2):
                    bank0 = 4 * (1 - half)
                    if half == 1:
                        pe.wait_ge(group_free, banked_before + FREE_AT_START)

                    def half_unit(b, s, r, opens=False, closes=False):
                        cut = slice(r * P, (r + 1) * P)
                        if r == 0:
                            n_unit = b * RING + s
                            pe.wait_ge(lo_ready, n_unit + ((first + half * bodies) * RING + 1 + RING))
                            pe.wait_ge(a_lo_ready, n_unit + (count + half * bodies * RING + 1))
                        last = closes and s == RING - 1
                        order = [(n, part) for part in ((0, 0), (0, 1), (1, 0)) for n in range(2)]
                        if last and half == 1 and r == 1:
                            order.sort(key=lambda item: item[0])
                        for n, (a_part, w_part) in order:
                            ins = mm(ps[:, bank0 + 2 * r + n, :], aT[:, s, a_part, cut],
                                     w[:, s, 2 * n:2 * n + 2, w_part, :],
                                     start=opens and s == 0 and a_part == 0 and w_part == 0,
                                     stop=last and a_part == 1)
                            if last and half == 1 and r == 1 and (n, a_part) == (0, 1):
                                did(ins, E, "row1_1")
                        if last and r == 0:
                            did(ins, E, f"row0_{half}")
                        if r == ROWS - 1:
                            ins.then_inc(unit_used, 1)

                    def body(b, **ends):
                        for s in range(RING):
                            for r in range(ROWS):
                                half_unit(b, s, r, **ends)

                    body(0, opens=True)
                    with pe.Fori(1, bodies - 1) as b:
                        body(b)
                    for r in range(ROWS):
                        for s in range(RING):
                            half_unit(bodies - 1, s, r, closes=True)

            after(pe, A1, "i_tanh1", H - 1)
            contraction(G_OUT, OUT_BODIES, 0, G_OUT, EO)
            n_up = G_UP - NOT_BANKED
            first_group(A2, V2, E2, G_UP, n_up)
            with pe.Fori(0, UP_ITERS - 1) as j:
                group(j * 2 + (G_UP + 1), j * 2 + (n_up + 1), 1)
                group(j * 2 + (G_UP + 2), j * 2 + (n_up + 2), 0)
            group(G_DOWN - 1, n_up + 2 * UP_ITERS - 1, 1)
            contraction(G_DOWN, DOWN_BODIES, 2 * KT, G_DOWN - NOT_BANKED, ED)


_WEIGHTS = ["w_in", "w_out", "w_up", "w_down"]


def kernel(**inputs):
    import numpy as np
    import concourse.bacc as bacc
    from concourse.bass_utils import run_bass_kernel_spmd

    a = {k: np.asarray(v) for k, v in inputs.items()}

    def cols(v, n):
        return v.reshape(n, P).T

    lru = np.stack([cols(t, LBLK) for t in (*a["lru_conv_w"][0], a["lru_conv_b"][0], a["lru_ba"][0], a["lru_bx"][0],
                                            a["lru_lambda"][0])], axis=2)
    ffn = np.stack([cols(t, FT) for t in (*a["ffn_conv_w"][0], a["ffn_conv_b"][0])], axis=2)
    bias = np.zeros((P, 1), np.float32)
    bias[0:H, 0] = a["b_gate_m"][0, :H]
    bias[F_ROW:F_ROW + H, 0] = a["b_gate_m"][0, H:]
    par = np.concatenate([cols(a["norm_mix_g"][0], KT), cols(a["norm_ffn_g"][0], KT),
                          cols(a["mlstm_norm_g"][0].reshape(-1), 2 * H),
                          lru.reshape(P, -1), ffn.reshape(P, -1), bias], axis=1)
    gate = a["w_in"][0][:, 4 * D_M:4 * D_M + 2 * H].reshape(KT, P, 2, H).transpose(1, 0, 2, 3)
    const = np.zeros((P, NCONST), np.float32)
    const[:, C_ID:C_ID + P] = np.eye(P)
    const[:, C_TRI:C_TRI + P] = np.triu(np.ones((P, P)))
    arrays = {"x": a["x"], **{n: a[n][0] for n in _WEIGHTS}, "wa": a["lru_wa"][0], "wx": a["lru_wx"][0],
              "gate_w": np.ascontiguousarray(gate), "par": par, "const": const, "gfin": a["norm_final_g"].reshape(1, D)}
    nc = bacc.Bacc("TRN2", target_bir_lowering=False, num_devices=1)
    in_map, args = {}, []
    for name, array in arrays.items():
        in_map[f"{name}_dram"] = np.ascontiguousarray(array)
        args.append(nc.dram_tensor(f"{name}_dram", array.shape, F32, kind="ExternalInput").ap())
    y = nc.dram_tensor("y_dram", (1, S, D), F32, kind="ExternalOutput").ap()
    hybrid_block(nc, *args, y)
    result = run_bass_kernel_spmd(nc, [in_map], core_ids=[0])
    return result.results[0]["y_dram"]
```
